# Optimizing a Trainium2 kernel written in Bass

```python
import jax
import jax.numpy as jnp
from jax import lax
import numpy as np

D_MODEL = 1024
BATCH = 1
SEQ = 256
DEPTH = 1

ATTN_HEADS = 8
ATTN_HEAD_DIM = 64
ATTN_WIDTH = ATTN_HEADS * ATTN_HEAD_DIM
MOBA_BLOCK = 256
MOBA_TOP_K = 3
Q_BLOCK = 128
MLSTM_HEADS = 4
MLSTM_HEAD_DIM = 128
MLSTM_WIDTH = MLSTM_HEADS * MLSTM_HEAD_DIM
MLSTM_CHUNK = 128
CONV_WIDTH = 4
FFN_HIDDEN = -(-8 * D_MODEL // (3 * 256)) * 256
NORM_EPS = 1e-6
IN_SPLITS = (ATTN_WIDTH, ATTN_WIDTH, ATTN_WIDTH,
             MLSTM_WIDTH, MLSTM_WIDTH, MLSTM_WIDTH, MLSTM_WIDTH,
             MLSTM_HEADS, MLSTM_HEADS, D_MODEL, D_MODEL)
IN_WIDTH = sum(IN_SPLITS)

kernel_name = 'hybrid_moba_mlstm_swiglu'

def rms_norm(x, g):
    xf = x.astype(jnp.float32)
    y = xf * lax.rsqrt(jnp.mean(xf * xf, axis=-1, keepdims=True) + NORM_EPS)
    return (y * g.astype(jnp.float32)).astype(x.dtype)

def to_heads(t, n_heads):
    b, s, w = t.shape
    return t.reshape(b, s, n_heads, w // n_heads).transpose(0, 2, 1, 3)

def from_heads(t):
    b, h, s, d = t.shape
    return t.transpose(0, 2, 1, 3).reshape(b, s, h * d)

def causal_depthwise_conv(x, w):
    width = w.shape[0]
    s = x.shape[1]
    xp = jnp.pad(x, ((0, 0), (width - 1, 0), (0, 0)))
    y = xp[:, 0:s] * w[0]
    for j in range(1, width):
        y = y + xp[:, j:j + s] * w[j]
    return y

def moba_attention(q, k, v, slopes):
    b, h, s, d = q.shape
    n_blk = -(-s // MOBA_BLOCK)
    s_pad = n_blk * MOBA_BLOCK
    pad = ((0, 0), (0, 0), (0, s_pad - s), (0, 0))
    k_pad = jnp.pad(k, pad)
    v_pad = jnp.pad(v, pad)
    k_blk = k_pad.reshape(b, h, n_blk, MOBA_BLOCK, d)
    v_blk = v_pad.reshape(b, h, n_blk, MOBA_BLOCK, d)
    k_mean = jnp.mean(k_blk.astype(jnp.float32), axis=3)
    top_k = min(MOBA_TOP_K, n_blk)
    n_sel = top_k * MOBA_BLOCK
    n_q = s // Q_BLOCK
    q_chunks = jnp.moveaxis(q.reshape(b, h, n_q, Q_BLOCK, d), 2, 0)
    b_ix = jnp.arange(b)[:, None, None, None]
    h_ix = jnp.arange(h)[None, :, None, None]
    blk_ids = jnp.arange(n_blk)
    key_off = jnp.arange(MOBA_BLOCK)
    scale = d ** -0.5
    slope = slopes[None, :, None, None]

    def one_block(args):
        q_i, q_blk = args
        t = q_blk * Q_BLOCK + jnp.arange(Q_BLOCK)
        own = (q_blk * Q_BLOCK) // MOBA_BLOCK
        qf = q_i.astype(jnp.float32)
        gate = jnp.einsum('bhqd,bhnd->bhqn', qf, k_mean)
        gate = jnp.where(blk_ids < own, gate, -jnp.inf)
        _, idx = lax.top_k(gate, top_k)
        k_sel = k_blk[b_ix, h_ix, idx].reshape(b, h, Q_BLOCK, n_sel, d)
        v_sel = v_blk[b_ix, h_ix, idx].reshape(b, h, Q_BLOCK, n_sel, d)
        pos_sel = (idx[..., None] * MOBA_BLOCK + key_off).reshape(b, h, Q_BLOCK, n_sel)
        valid_sel = jnp.repeat(jnp.arange(top_k) < own, MOBA_BLOCK)
        s_sel = jnp.einsum('bhqd,bhqkd->bhqk', qf, k_sel.astype(jnp.float32)) * scale
        s_sel = s_sel - slope * (t[:, None] - pos_sel)
        s_sel = jnp.where(valid_sel, s_sel, -jnp.inf)
        k_own = lax.dynamic_slice_in_dim(k_pad, own * MOBA_BLOCK, MOBA_BLOCK, axis=2)
        v_own = lax.dynamic_slice_in_dim(v_pad, own * MOBA_BLOCK, MOBA_BLOCK, axis=2)
        pos_own = own * MOBA_BLOCK + key_off
        s_own = jnp.einsum('bhqd,bhkd->bhqk', qf, k_own.astype(jnp.float32)) * scale
        s_own = s_own - slope * (t[:, None] - pos_own[None, :])
        s_own = jnp.where(pos_own[None, :] <= t[:, None], s_own, -jnp.inf)
        p = jax.nn.softmax(jnp.concatenate([s_sel, s_own], axis=-1), axis=-1)
        o = (jnp.einsum('bhqk,bhqkd->bhqd', p[..., :n_sel], v_sel.astype(jnp.float32))
             + jnp.einsum('bhqk,bhkd->bhqd', p[..., n_sel:], v_own.astype(jnp.float32)))
        return o.astype(q.dtype)

    out = lax.map(one_block, (q_chunks, jnp.arange(n_q)))
    return jnp.moveaxis(out, 0, 2).reshape(b, h, s, d)

def mlstm_chunkwise(q, k, v, log_i, log_f):
    b, h, s, d = q.shape
    L = MLSTM_CHUNK
    nc = s // L

    def chunks(t):
        return jnp.moveaxis(t.reshape((b, h, nc, L) + t.shape[3:]), 2, 0)

    qf = q.astype(jnp.float32)
    kf = k.astype(jnp.float32) * (d ** -0.5)
    vf = v.astype(jnp.float32)
    bcum = jnp.moveaxis(jnp.cumsum(log_f.reshape(b, h, nc, L), axis=-1), 2, 0)
    causal = jnp.tril(jnp.ones((L, L), dtype=bool))

    def step(carry, xs):
        C, n, m = carry
        qc, kc, vc, ic, bc = xs
        dmat = bc[..., :, None] - bc[..., None, :] + ic[..., None, :]
        dmat = jnp.where(causal, dmat, -jnp.inf)
        inter = bc + m[..., None]
        m_t = jnp.maximum(inter, jnp.max(dmat, axis=-1))
        w_intra = jnp.exp(dmat - m_t[..., None])
        w_inter = jnp.exp(inter - m_t)
        sc = jnp.einsum('bhtd,bhsd->bhts', qc, kc) * w_intra
        num = (w_inter[..., None] * jnp.einsum('bhtd,bhde->bhte', qc, C)
               + jnp.einsum('bhts,bhse->bhte', sc, vc))
        den = w_inter * jnp.einsum('bhtd,bhd->bht', qc, n) + jnp.sum(sc, axis=-1)
        h_out = num / jnp.maximum(jnp.abs(den), jnp.exp(-m_t))[..., None]
        b_last = bc[..., -1]
        g = b_last[..., None] - bc + ic
        m_new = jnp.maximum(b_last + m, jnp.max(g, axis=-1))
        w_s = jnp.exp(g - m_new[..., None])
        decay = jnp.exp(b_last + m - m_new)
        C = decay[..., None, None] * C + jnp.einsum('bhs,bhsd,bhse->bhde', w_s, kc, vc)
        n = decay[..., None] * n + jnp.einsum('bhs,bhsd->bhd', w_s, kc)
        return (C, n, m_new), h_out

    init = (jnp.zeros((b, h, d, d), jnp.float32),
            jnp.zeros((b, h, d), jnp.float32),
            jnp.zeros((b, h), jnp.float32))
    _, hs = lax.scan(step, init, (chunks(qf), chunks(kf), chunks(vf), chunks(log_i), bcum))
    return jnp.moveaxis(hs, 0, 2).reshape(b, h, s, d)

def head_layer_norm(h, g):
    mu = jnp.mean(h, axis=-1, keepdims=True)
    var = jnp.mean(jnp.square(h - mu), axis=-1, keepdims=True)
    nh, dh = h.shape[1], h.shape[3]
    return (h - mu) * lax.rsqrt(var + NORM_EPS) * g.astype(jnp.float32).reshape(nh, dh)[None, :, None, :]

def setup_inputs(seed: int = 0) -> dict:
    key = jax.random.key(seed)
    ks = jax.random.split(key, 16)
    f32 = jnp.float32
    nrm = lambda k, shp: jax.random.normal(k, shp, f32)
    return {
        'x': nrm(ks[0], (BATCH, SEQ, D_MODEL)),
        'mix_norm_g': 1.0 + 0.02 * nrm(ks[1], (DEPTH, D_MODEL)),
        'w_in': nrm(ks[2], (DEPTH, D_MODEL, IN_WIDTH)) * D_MODEL ** -0.5,
        'conv_qk': nrm(ks[3], (DEPTH, CONV_WIDTH, 2 * MLSTM_WIDTH)) * CONV_WIDTH ** -0.5,
        'b_igate': 0.1 * nrm(ks[4], (DEPTH, MLSTM_HEADS)),
        'b_fgate': jnp.linspace(3.0, 6.0, MLSTM_HEADS, dtype=f32)[None, :] + 0.1 * nrm(ks[5], (DEPTH, MLSTM_HEADS)),
        'mlstm_norm_g': 1.0 + 0.02 * nrm(ks[6], (DEPTH, MLSTM_WIDTH)),
        'w_out_attn': nrm(ks[7], (DEPTH, ATTN_WIDTH, D_MODEL)) * ATTN_WIDTH ** -0.5,
        'w_out_mlstm': nrm(ks[8], (DEPTH, MLSTM_WIDTH, D_MODEL)) * MLSTM_WIDTH ** -0.5,
        'w_o': nrm(ks[9], (DEPTH, D_MODEL, D_MODEL)) * D_MODEL ** -0.5,
        'ffn_norm_g': 1.0 + 0.02 * nrm(ks[10], (DEPTH, D_MODEL)),
        'w_ffn_gate': nrm(ks[11], (DEPTH, D_MODEL, FFN_HIDDEN)) * D_MODEL ** -0.5,
        'w_ffn_up': nrm(ks[12], (DEPTH, D_MODEL, FFN_HIDDEN)) * D_MODEL ** -0.5,
        'w_ffn_down': nrm(ks[13], (DEPTH, FFN_HIDDEN, D_MODEL)) * FFN_HIDDEN ** -0.5,
        'final_norm_g': 1.0 + 0.02 * nrm(ks[14], (D_MODEL,)),
    }

def reference(x, mix_norm_g, w_in, conv_qk, b_igate, b_fgate, mlstm_norm_g,
              w_out_attn, w_out_mlstm, w_o, ffn_norm_g, w_ffn_gate, w_ffn_up,
              w_ffn_down, final_norm_g):
    f32 = jnp.float32
    slopes = jnp.exp2(-8.0 * jnp.arange(1, ATTN_HEADS + 1, dtype=f32) / ATTN_HEADS)
    split_points = np.cumsum(IN_SPLITS)[:-1].tolist()
    for layer in range(DEPTH):
        h = rms_norm(x, mix_norm_g[layer])
        proj = h @ w_in[layer]
        (q_a, k_a, v_a, q_m, k_m, v_m, o_m, i_m, f_m, g_a, g_m) = jnp.split(proj, split_points, axis=-1)
        y_a = from_heads(moba_attention(to_heads(q_a, ATTN_HEADS), to_heads(k_a, ATTN_HEADS),
                                        to_heads(v_a, ATTN_HEADS), slopes))
        qk_m = jax.nn.silu(causal_depthwise_conv(jnp.concatenate([q_m, k_m], axis=-1), conv_qk[layer]))
        q_m, k_m = jnp.split(qk_m, 2, axis=-1)
        log_i = (i_m.astype(f32) + b_igate[layer].astype(f32)).transpose(0, 2, 1)
        log_f = jax.nn.log_sigmoid(f_m.astype(f32) + b_fgate[layer].astype(f32)).transpose(0, 2, 1)
        h_m = mlstm_chunkwise(to_heads(q_m, MLSTM_HEADS), to_heads(k_m, MLSTM_HEADS),
                              to_heads(v_m, MLSTM_HEADS), log_i, log_f)
        h_m = h_m * jax.nn.sigmoid(to_heads(o_m, MLSTM_HEADS).astype(f32))
        y_m = from_heads(head_layer_norm(h_m, mlstm_norm_g[layer])).astype(x.dtype)
        merged = (jax.nn.sigmoid(g_a) * (y_a @ w_out_attn[layer])
                  + jax.nn.sigmoid(g_m) * (y_m @ w_out_mlstm[layer]))
        x = x + merged @ w_o[layer]
        h = rms_norm(x, ffn_norm_g[layer])
        x = x + (jax.nn.silu(h @ w_ffn_gate[layer]) * (h @ w_ffn_up[layer])) @ w_ffn_down[layer]
    return rms_norm(x, final_norm_g)


_drawn_inputs = setup_inputs


def setup_inputs(seed=0):
    import zlib

    import numpy as np

    out = dict(_drawn_inputs(seed))
    spreads = {}
    factors = {'mix_norm_g': 2.738,
     'b_igate': 64.0,
     'mlstm_norm_g': 5.43,
     'ffn_norm_g': 4.402,
     'final_norm_g': 8.265}
    for name, (base, spread) in spreads.items():
        noise = np.random.default_rng([zlib.crc32(name.encode()), seed]).standard_normal(out[name].shape)
        drawn = base * np.exp(spread * noise) if base else spread * noise
        out[name] = jnp.asarray(drawn.astype(out[name].dtype))
    for name, factor in factors.items():
        out[name] = (out[name] * factor).astype(out[name].dtype)
    return out
```

```python
from contextlib import ExitStack

import concourse.bass as bass
from concourse import mybir

ALU = mybir.AluOpType
ACT = mybir.ActivationFunctionType
F32 = mybir.dt.float32
F32R = mybir.dt.float32r
BF16 = mybir.dt.bfloat16

P = 128
S = 256
T = S // P
D = 1024
KT = D // P
H_A, D_A = 8, 64
H_M, D_M = 4, 128
W_A, W_M = H_A * D_A, H_M * D_M
CONV = 4
F = 2816
EPS = 1e-6
MASKED = -1e30
LOWEST = -3.0e38

Q_A, K_A, V_A = 0, W_A, 2 * W_A
Q_M = 3 * W_A
K_M, V_M, O_M = Q_M + W_M, Q_M + 2 * W_M, Q_M + 3 * W_M
I_M = Q_M + 4 * W_M
G_A = I_M + 2 * H_M
G_M = G_A + D

CH = 2048
RAW = 3
RING = 6
BLOCKS = [Q_M, K_M, Q_A, K_A, V_A, V_M, O_M, G_A, G_A + 512, G_M, G_M + 512]
FEATURE_MAJOR = 4
NB = len(BLOCKS)
C_OUT = 2 * NB
C_WO = C_OUT + 4
C_FFN = C_WO + 4
FG = F // 256
FIRST = 0
AHEAD = 4


def slot_of(c):
    return c % RING


def build(nc, x, mix_norm_g, w_in, conv_qk, b_igate, b_fgate, mlstm_norm_g, w_out_attn,
          w_out_mlstm, w_o, ffn_norm_g, w_ffn_gate, w_ffn_up, w_ffn_down, final_norm_g, out):
    x_d = x[0].rearrange("(t p) n -> p t n", p=P)
    out_d = out[0].rearrange("(t p) n -> p t n", p=P)
    w_in_k = w_in[0].rearrange("(k p) n -> p k n", p=P)
    wo_k = w_o[0].rearrange("(k p) n -> p k n", p=P)
    woa_k = w_out_attn[0].rearrange("(k p) n -> p k n", p=P)
    wom_k = w_out_mlstm[0].rearrange("(k p) n -> p k n", p=P)
    gate_k = w_ffn_gate[0].rearrange("(k p) n -> p k n", p=P)
    up_k = w_ffn_up[0].rearrange("(k p) n -> p k n", p=P)
    down_k = w_ffn_down[0].rearrange("(k p) n -> p k n", p=P)

    with ExitStack() as ctx:
        def sb(name, shape, dt=F32):
            return ctx.enter_context(nc.sbuf_tensor(name, shape, dt))

        def sem(name):
            return ctx.enter_context(nc.semaphore(name))

        w_raw = sb("w_raw", [P, RAW, CH])
        w_hi = sb("w_hi", [P, RING, CH], F32R)
        w_lo = sb("w_lo", [P, RING, CH], F32R)
        hT_hi = sb("hT_hi", [P, KT, S], F32R)
        hT_lo = sb("hT_lo", [P, KT, S], F32R)
        yT_hi = sb("yT_hi", [P, 8, S], F32R)
        yT_lo = sb("yT_lo", [P, 8, S], F32R)
        wif_hi = sb("wif_hi", [P, KT, 36], F32R)
        wif_lo = sb("wif_lo", [P, KT, 36], F32R)
        x_sb = sb("x_sb", [P, T * D])
        region_a = sb("region_a", [P, T * D])
        region_b = sb("region_b", [P, T * D])
        v_att = sb("v_att", [P, T * W_A])
        v_ml = sb("v_ml", [P, T * H_M * (D_M + 1)])
        o_sb = sb("o_sb", [P, T * W_M])
        w_ml = sb("w_ml", [P, H_M * 384])
        pT = sb("pT", [P, 2, 384])
        alibi = sb("alibi", [P, H_A, 384], BF16)
        ident = sb("ident", [P, P])
        vcol = sb("vcol", [P, 36])
        sumsq = sb("sumsq", [P, 6])
        meansq = sb("meansq", [P, 6])
        rstd = sb("rstd", [P, 6])
        minus_half = sb("minus_half", [P, 8])
        b_if = sb("b_if", [H_M, 2])
        rcol = sb("rcol", [P, 16])
        smax = sb("smax", [P, 16])
        nsmax = sb("nsmax", [P, 16])
        ssum = sb("ssum", [P, 16])
        sinv = sb("sinv", [P, 16])
        den = sb("den", [P, 8])
        dinv = sb("dinv", [P, 8])
        bn = sb("bn", [P, 8, 6])
        mv = sb("mv", [P, 8, 2])
        lnv = sb("lnv", [P, 8])
        lnr = sb("lnr", [P, 8])

        x_t = x_sb[:, :].rearrange("p (t n) -> p t n", t=T)
        prob = x_sb[:, 0:1536].rearrange("p (s e n) -> p s e n", s=2, e=2)
        ra_t = region_a[:, :].rearrange("p (t n) -> p t n", t=T)
        rb_t = region_b[:, :].rearrange("p (t n) -> p t n", t=T)
        qk_m = region_a[:, :].rearrange("p (f n) -> p f n", f=8)
        qk_a = region_b[:, :].rearrange("p (f n) -> p f n", f=8)
        hid = region_a[:, 0:1024].rearrange("p (s n) -> p s n", s=2)
        va = v_att[:, :].rearrange("p (t n) -> p t n", t=T)
        vm = v_ml[:, :].rearrange("p (t h n) -> p t h n", t=T, h=H_M)
        o_t = o_sb[:, :].rearrange("p (t n) -> p t n", t=T)
        wm = w_ml[:, :].rearrange("p (h n) -> p h n", h=H_M)
        gain_ffn = v_att[:, 0:D]
        gain_fin = v_ml[:, 0:D]
        gmix_row = v_ml[0:1, 0:D]
        vec_rows = pT[0:36, 1, 128:256]
        row_i, row_f, row_l, row_b = (o_sb[0:H_M, n * S:(n + 1) * S] for n in range(4))
        row_m, row_e = (v_ml[0:H_M, n * S:(n + 1) * S] for n in range(2))
        row_one = w_ml[0:H_M, 0:S]
        ones_row = w_ml[0:1, 256:384]
        wif_pad = w_ml[:, 512:512 + KT * 36].rearrange("p (k n) -> p k n", k=KT)
        wif_raw = w_ml[:, 1024:1024 + KT * 8].rearrange("p (k n) -> p k n", k=KT)
        dist = w_ml[:, 1100:1100 + 384]
        sel = pT[0:H_M, :, :].rearrange("p e n -> p (e n)")[:, 0:512]

        pp = ctx.enter_context(nc.psum_tensor("pp", [P, 4, 512], F32))
        pa = ctx.enter_context(nc.psum_tensor("pa", [P, 4, 512], F32))

        x_loaded = [sem(f"x_loaded{t}") for t in range(T)]
        gmix_loaded = sem("gmix_loaded")
        vec_loaded = sem("vec_loaded")
        wif_loaded = sem("wif_loaded")
        bif_loaded = sem("bif_loaded")
        gain_ffn_loaded = sem("gain_ffn_loaded")
        gain_fin_loaded = sem("gain_fin_loaded")
        x_reloaded = sem("x_reloaded")
        chunk_loaded = [sem(f"chunk_loaded{s}") for s in range(RAW)]
        hi_ready = sem("hi_ready")
        lo_ready = sem("lo_ready")
        chunk_used = sem("chunk_used")
        ones_set = sem("ones_set")
        pool_step = sem("pool_step")
        ident_set = sem("ident_set")
        wif_zeroed = sem("wif_zeroed")
        sel_set = sem("sel_set")
        alibi_set = sem("alibi_set")
        sumsq_done = sem("sumsq_done")
        rstd_done = sem("rstd_done")
        normed = sem("normed")
        gmix_spread = sem("gmix_spread")
        vec_turned = sem("vec_turned")
        vcol_set = sem("vcol_set")
        turned = sem("turned")
        hT_hi_set = sem("hT_hi_set")
        hT_lo_set = sem("hT_lo_set")
        wif_hi_set = sem("wif_hi_set")
        wif_lo_set = sem("wif_lo_set")
        wif_padded = sem("wif_padded")
        tile0_done = sem("tile0_done")
        proj_free = [sem(f"proj_free{s}") for s in range(2)]
        tap3_done = sem("tap3_done")
        conv_step = sem("conv_step")
        silu_done = sem("silu_done")
        gates_done = sem("gates_done")
        gate_rows_set = sem("gate_rows_set")
        log_done = sem("log_done")
        exp1_done = sem("exp1_done")
        scans_done = sem("scans_done")
        exp_m_done = sem("exp_m_done")
        cols_turned = sem("cols_turned")
        m_spread = sem("m_spread")
        rcol_set = sem("rcol_set")
        w_exp_done = sem("w_exp_done")
        w_masked = sem("w_masked")
        qk_m_done = sem("qk_m_done")
        w_ready = sem("w_ready")
        v_ml_set = sem("v_ml_set")
        scores_done = sem("scores_done")
        scores_read = sem("scores_read")
        nsmax_set = sem("nsmax_set")
        exp_done = sem("exp_done")
        prob_ready = sem("prob_ready")
        prob_turned = sem("prob_turned")
        pT_set = sem("pT_set")
        pv_done = sem("pv_done")
        ya_hi_set = sem("ya_hi_set")
        ya_lo_set = sem("ya_lo_set")
        num_done = sem("num_done")
        num_read = sem("num_read")
        var_set = sem("var_set")
        lnr_set = sem("lnr_set")
        y_normed = sem("y_normed")
        ym_turned = sem("ym_turned")
        ym_hi_set = sem("ym_hi_set")
        ym_lo_set = sem("ym_lo_set")
        wout_done = sem("wout_done")
        merged = sem("merged")
        wo_done = sem("wo_done")
        x2_ready = sem("x2_ready")
        silu_f_done = sem("silu_f_done")
        prod_done = sem("prod_done")
        a_hi_set = sem("a_hi_set")
        a_lo_set = sem("a_lo_set")
        ffn_out_done = sem("ffn_out_done")
        x3_ready = sem("x3_ready")
        out_ready = sem("out_ready")
        stored = sem("stored")
        dve_step = sem("dve_step")

        block = ctx.enter_context(nc.Block())

        def chunk_source(c):
            if c < C_OUT:
                b, h = divmod(c, 2)
                if b < FEATURE_MAJOR:
                    return w_in_k[:, :, BLOCKS[b] + 256 * h:BLOCKS[b] + 256 * (h + 1)]
                return w_in_k[:, 4 * h:4 * h + 4, BLOCKS[b]:BLOCKS[b] + 512]
            if c < C_WO:
                w = woa_k if c < C_OUT + 2 else wom_k
                n = (c - C_OUT) % 2
                return w[:, :, 512 * n:512 * (n + 1)]
            if c < C_FFN:
                n, h = divmod(c - C_WO, 2)
                return wo_k[:, 4 * h:4 * h + 4, 512 * n:512 * (n + 1)]
            return (gate_k, up_k)[c - C_FFN][:, :, 0:256]

        def as_source(ap, src):
            return ap.rearrange("p (k n) -> p k n", n=src.shape[-1])

        @block.sync
        def _(sp):
            def load(c, src):
                if c >= RAW:
                    sp.wait_ge(lo_ready, c - RAW + 1)
                sp.dma_start(as_source(w_raw[:, c % RAW, :], src), src).then_inc(chunk_loaded[c % RAW], 16)

            sp.dma_start(x_t[:, 0], x_d[:, 0]).then_inc(x_loaded[0], 16)
            sp.dma_start(x_t[:, 1], x_d[:, 1]).then_inc(x_loaded[1], 16)
            for c in range(C_FFN + 2):
                load(c, chunk_source(c))
                if c == 1:
                    with nc.allow_non_contiguous_dma(reason="eight gate columns"):
                        sp.dma_start(wif_raw, w_in_k[:, :, I_M:I_M + 2 * H_M]).then_inc(wif_loaded, 16)
                if c == 25:
                    sp.wait_ge(prob_turned, H_A // 2)
                    sp.dma_start(x_sb[:, :].rearrange("p (t n) -> p t n", t=T), x_d).then_inc(x_reloaded, 16)
                    sp.wait_ge(pv_done, H_A // 2)
                    sp.dma_start(gain_ffn, ffn_norm_g[0:1, :].to_broadcast([P, D])).then_inc(gain_ffn_loaded, 16)
                    sp.wait_ge(num_done, H_M)
                    sp.dma_start(gain_fin, final_norm_g.rearrange("(a n) -> a n", a=1).to_broadcast([P, D])
                                 ).then_inc(gain_fin_loaded, 16)
            with sp.Fori(0, (FG - 1) // 2) as i:
                for j in range(2):
                    c = C_FFN + 2 + 3 * j
                    srcs = (gate_k[:, :, bass.ds(i * 512 + 256 * (1 + j), 256)],
                            up_k[:, :, bass.ds(i * 512 + 256 * (1 + j), 256)],
                            down_k[:, bass.ds(i * 4 + 2 * j, 2), :])
                    for r, src in enumerate(srcs):
                        slot = (c + r) % RAW
                        sp.wait_ge(lo_ready, i * 6 + (c + r - RAW + 1))
                        n = 1024 if r == 2 else 256
                        sp.dma_start(w_raw[:, slot, :].rearrange("p (k n) -> p k n", n=n), src
                                     ).then_inc(chunk_loaded[slot], 16)
            c = C_FFN + 2 + 3 * (FG - 1)
            load(c, down_k[:, 2 * (FG - 1):2 * FG, :])
            for t in range(T):
                sp.wait_ge(out_ready, t + 1)
                sp.dma_start(out_d[:, t], rb_t[:, t]).then_inc(stored, 16)
            sp.wait_ge(stored, 16 * T)

        @block.gpsimd
        def _(pool):
            steps = [0]

            def link(ins):
                steps[0] += 1
                ins.then_inc(pool_step, 1)
                pool.wait_ge(pool_step, steps[0])

            def rsqrt(n):
                pool.wait_ge(sumsq_done, n + 1)
                link(nc.gpsimd.tensor_scalar(meansq[:, n:n + 1], sumsq[:, n:n + 1], 1.0 / D, EPS,
                                             ALU.mult, ALU.add))
                nc.gpsimd.tensor_tensor(rstd[:, n:n + 1], meansq[:, n:n + 1], minus_half[:, 0:1],
                                        ALU.pow).then_inc(rstd_done, 1)

            nc.gpsimd.memset(ones_row, 1.0).then_inc(ones_set, 1)
            link(nc.gpsimd.memset(minus_half[:, :], -0.5))
            link(nc.gpsimd.memset(ident[:, :], 0.0))
            nc.gpsimd.affine_select(out=ident[:, :], in_=ident[:, :], compare_op=ALU.not_equal, fill=1.0,
                                    base=0, pattern=[[-1, P]], channel_multiplier=1).then_inc(ident_set, 1)
            nc.gpsimd.memset(wif_pad, 0.0).then_inc(wif_zeroed, 1)
            for t in range(T):
                rsqrt(t)
            nc.gpsimd.memset(row_one, 1.0).then_inc(ones_set, 1)
            link(nc.gpsimd.memset(sel, 0.0))
            nc.gpsimd.affine_select(out=sel.rearrange("p (h n) -> p h n", h=H_M),
                                    in_=sel.rearrange("p (h n) -> p h n", h=H_M),
                                    compare_op=ALU.not_equal, fill=-1.0, base=0,
                                    pattern=[[-1, H_M], [0, P]], channel_multiplier=1).then_inc(sel_set, 1)
            link(nc.gpsimd.iota(dist[:, 0:128], pattern=[[1, 128]], base=0, channel_multiplier=-1,
                                allow_small_or_imprecise_dtypes=True))
            link(nc.gpsimd.iota(dist[:, 128:384], pattern=[[1, 256]], base=-128, channel_multiplier=-1,
                                allow_small_or_imprecise_dtypes=True))
            for h in range(H_A):
                slope = 2.0 ** (-8.0 * (h + 1) / H_A)
                ins = nc.gpsimd.tensor_scalar(alibi[:, h, :], dist, slope * D_A ** 0.5, None, ALU.mult)
            link(ins)
            for lo in (0, 256):
                part = alibi[:, :, lo:lo + 128]
                nc.gpsimd.affine_select(out=part, in_=part, compare_op=ALU.is_ge, fill=MASKED, base=0,
                                        pattern=[[0, H_A], [-1, 128]], channel_multiplier=1
                                        ).then_inc(alibi_set, 1)
            pool.wait_ge(w_exp_done, 2 * H_M)
            for lo in (0, 256):
                part = wm[:, :, lo:lo + 128]
                nc.gpsimd.affine_select(out=part, in_=part, compare_op=ALU.is_ge, fill=0.0, base=0,
                                        pattern=[[0, H_M], [1, 128]], channel_multiplier=-1
                                        ).then_inc(w_masked, 1)
            pool.wait_ge(var_set, H_M)
            link(nc.gpsimd.tensor_scalar(lnv[:, :], mv[:, :, 1], EPS, None, ALU.add))
            nc.gpsimd.tensor_tensor(lnr[:, :], lnv[:, :], minus_half[:, :], ALU.pow).then_inc(lnr_set, 1)
            for n in range(2, 6):
                rsqrt(n)

        @block.scalar
        def _(act):
            def split_hi(c):
                act.wait_ge(chunk_loaded[c % RAW], 16 * (c // RAW + 1))
                if c >= RING:
                    act.wait_ge(chunk_used, c - RING + 1)
                nc.scalar.activation(w_hi[:, slot_of(c), :], w_raw[:, c % RAW, :], ACT.Copy).then_inc(hi_ready, 1)

            def square(n, src, wait, value):
                act.wait_ge(wait, value)
                if n:
                    act.wait_ge(sumsq_done, n)
                nc.scalar.activation(o_sb[:, :], src, ACT.Square, accum_out=sumsq[:, n:n + 1]
                                     ).then_inc(sumsq_done, 1)

            def turn_hi(e, t, banks):
                for b, bank in enumerate(banks):
                    act.wait_ge(turned, 2 * e + b + 1)
                    nc.scalar.activation(hT_hi[:, 4 * b:4 * b + 4, t * P:(t + 1) * P],
                                         bank.rearrange("p (k n) -> p k n", k=4), ACT.Copy).then_inc(hT_hi_set, 1)

            def tap3(c):
                b, h = divmod(c, 2)
                act.wait_ge(chunk_used, c + 1)
                if c == 0:
                    act.wait_ge(vcol_set, 1)
                for f in range(2):
                    ft = 4 * b + 2 * h + f
                    col = 4 + 3 * 8 + ft
                    ins = nc.scalar.activation(qk_m[:, ft, :], pp[:, 2 * (b % 2) + h, f * S:(f + 1) * S],
                                               ACT.Copy, scale=vcol[:, col:col + 1])
                ins.then_inc(tap3_done, 1)

            def copy_qk(c):
                b, h = divmod(c, 2)
                act.wait_ge(chunk_used, c + 1)
                ft = 4 * (b - 2) + 2 * h
                nc.scalar.activation(qk_a[:, ft:ft + 2, :],
                                     pp[:, 2 * (b % 2) + h, :].rearrange("p (f n) -> p f n", f=2),
                                     ACT.Copy).then_inc(proj_free[b % 2], 1)

            def read_block(b, dst, func):
                for t in range(T):
                    if t == 0:
                        act.wait_ge(tile0_done, b - FEATURE_MAJOR + 1)
                    else:
                        act.wait_ge(chunk_used, 2 * b + 2)
                    nc.scalar.activation(dst(t), pp[:, 2 * (b % 2) + t, :], func).then_inc(proj_free[b % 2], 1)

            def softmax_exp(p):
                act.wait_ge(nsmax_set, p + 1)
                for e in range(2):
                    for lo, hi, q in ((0, 128, 0), (128, 384, 1)):
                        n = 4 * p + 2 * e + q
                        part = prob[:, p % 2, e, lo:hi]
                        ins = nc.scalar.activation(part, part, ACT.Exp, bias=nsmax[:, n:n + 1],
                                                   scale=D_A ** -0.5, accum_out=ssum[:, n:n + 1])
                ins.then_inc(exp_done, 1)

            def copy_pT(p):
                act.wait_ge(prob_turned, p + 1)
                if p:
                    act.wait_ge(pv_done, p)
                else:
                    act.wait_ge(m_spread, 1)
                for e in range(2):
                    ins = nc.scalar.activation(pT[:, e, :], pa[:, 2 + e, 0:384], ACT.Copy)
                ins.then_inc(pT_set, 1)

            def ya_hi(p):
                act.wait_ge(pv_done, p + 1)
                nc.scalar.activation(yT_hi[:, p, :], pa[:, 0, 0:S], ACT.Copy).then_inc(ya_hi_set, 1)

            act.dma_start(gmix_row, mix_norm_g[0:1, :]).then_inc(gmix_loaded, 16)
            act.dma_start(vec_rows[0:4, :], mlstm_norm_g.rearrange("a (h p) -> (a h) p", p=P)).then_inc(vec_loaded, 16)
            act.dma_start(vec_rows[4:36, :], conv_qk.rearrange("a j (f p) -> (a j f) p", p=P)).then_inc(vec_loaded, 16)
            with nc.allow_non_contiguous_dma(reason="four biases"):
                act.dma_start(b_if[:, 0:1], b_igate.rearrange("a h -> h a")).then_inc(bif_loaded, 16)
                act.dma_start(b_if[:, 1:2], b_fgate.rearrange("a h -> h a")).then_inc(bif_loaded, 16)
            square(0, x_t[:, 0], x_loaded[0], 16)
            square(1, x_t[:, 1], x_loaded[1], 16)
            split_hi(0)
            turn_hi(0, 0, (pa[:, 0, :], pa[:, 1, :]))
            turn_hi(1, 1, (pp[:, 2, :], pp[:, 3, :]))
            for c in range(1, AHEAD):
                split_hi(c)
            act.wait_ge(wif_padded, 2)
            nc.scalar.activation(wif_hi[:, :, :], wif_pad, ACT.Copy).then_inc(wif_hi_set, 1)

            for c in range(C_OUT):
                split_hi(c + AHEAD)
                if c == 2:
                    act.wait_ge(gate_rows_set, 1)
                    nc.scalar.activation(row_l, row_l, ACT.Exp).then_inc(exp1_done, 1)
                    act.wait_ge(exp1_done, 1)
                    nc.scalar.activation(row_l, row_l, ACT.Ln, bias=1.0).then_inc(log_done, 1)
                if c == 4:
                    act.wait_ge(scans_done, 1)
                    nc.scalar.activation(row_e, row_e, ACT.Exp, scale=-1.0).then_inc(exp_m_done, 1)
                    for n in range(4):
                        act.wait_ge(conv_step, 6 * (n + 1))
                        nc.scalar.activation(qk_m[:, 2 * n:2 * n + 2, :], qk_m[:, 2 * n:2 * n + 2, :],
                                             ACT.Silu).then_inc(silu_done, 1)
                if c == 6:
                    act.wait_ge(m_spread, 1)
                    act.wait_ge(rcol_set, 1)
                    act.wait_ge(alibi_set, 2)
                    for h in range(H_M):
                        neg_m = pa[:, 2 + h // 2, (h % 2) * S:(h % 2 + 1) * S]
                        nc.scalar.activation(wm[:, h, 0:S], neg_m, ACT.Exp, bias=rcol[:, h:h + 1]
                                             ).then_inc(w_exp_done, 1)
                        nc.scalar.activation(wm[:, h, S:384], neg_m[:, 128:256], ACT.Exp,
                                             bias=rcol[:, 4 + h:5 + h]).then_inc(w_exp_done, 1)
                if c in (10, 11):
                    softmax_exp(c - 10)
                if c == 12:
                    copy_pT(0)
                if c == 13:
                    ya_hi(0)
                    softmax_exp(2)
                if c == 14:
                    copy_pT(1)
                if c == 15:
                    ya_hi(1)
                    softmax_exp(3)
                    read_block(6, lambda t: o_t[:, t], ACT.Sigmoid)
                if c == 16:
                    copy_pT(2)
                if c == 17:
                    ya_hi(2)
                    copy_pT(3)
                if c == 18:
                    ya_hi(3)
                if c < 4:
                    tap3(c)
                elif c < 8:
                    copy_qk(c)
                elif c == 9:
                    read_block(4, lambda t: va[:, t], ACT.Copy)
                elif c in (16, 18, 20):
                    b = c // 2 - 1
                    dst = (ra_t, rb_t)[(b - 7) // 2]
                    read_block(b, lambda t: dst[:, t, ((b - 7) % 2) * 512:((b - 7) % 2 + 1) * 512], ACT.Sigmoid)
                if c == 20:
                    for b in range(2):
                        act.wait_ge(ym_turned, b + 1)
                        for f in range(2):
                            h = 2 * b + f
                            ins = nc.scalar.activation(yT_hi[:, 4 + h, :], pa[:, 2 + b, f * S:(f + 1) * S],
                                                       ACT.Copy, scale=vcol[:, h:h + 1])
                        ins.then_inc(ym_hi_set, 1)
            read_block(NB - 1, lambda t: rb_t[:, t, 512:1024], ACT.Sigmoid)
            for c in range(C_OUT + AHEAD, C_OUT + 8):
                split_hi(c)
            turn_hi(2, 0, (pa[:, 0, :], pa[:, 1, :]))
            for c in range(C_OUT + 8, C_FFN + 2):
                split_hi(c)
            turn_hi(3, 1, (pp[:, 0, :], pp[:, 1, :]))
            square(2, x_t[:, 0], x2_ready, 1)
            turn_hi(4, 0, (pa[:, 0, :], pa[:, 1, :]))
            square(3, x_t[:, 1], x2_ready, 2)
            turn_hi(5, 1, (pp[:, 0, :], pp[:, 1, :]))

            def hidden(i, g):
                act.wait_ge(chunk_used, i * 6 + (C_FFN + max(3 * g, 1)))
                if g >= 2 or i is not FIRST:
                    act.wait_ge(a_lo_set, i * 2 + (g - 1))
                nc.scalar.activation(hid[:, g % 2, :], pa[:, g % 2, :], ACT.Silu).then_inc(silu_f_done, 1)
                act.wait_ge(prod_done, i * 2 + g + 1)
                if g >= 2 or i is not FIRST:
                    act.wait_ge(chunk_used, i * 6 + (C_FFN + 3 * g - 1))
                nc.scalar.activation(yT_hi[:, 2 * (g % 2):2 * (g % 2) + 2, :],
                                     hid[:, g % 2, :].rearrange("p (f n) -> p f n", f=2), ACT.Copy
                                     ).then_inc(a_hi_set, 1)

            def two_groups(i):
                for j in range(2):
                    c = C_FFN + 2 + 3 * j
                    for r in range(3):
                        act.wait_ge(chunk_loaded[(c + r) % RAW], i * 32 + 16 * ((c + r) // RAW + 1))
                        act.wait_ge(chunk_used, i * 6 + (c + r - RING + 1))
                        nc.scalar.activation(w_hi[:, slot_of(c + r), :], w_raw[:, (c + r) % RAW, :], ACT.Copy
                                             ).then_inc(hi_ready, 1)
                    hidden(i, 1 + j)

            hidden(FIRST, 0)
            two_groups(FIRST)
            with act.Fori(1, (FG - 1) // 2) as i:
                two_groups(i)
            split_hi(C_FFN + 2 + 3 * (FG - 1))
            square(4, x_t[:, 0], x3_ready, 1)
            square(5, x_t[:, 1], x3_ready, 2)

        @block.vector
        def _(dve):
            steps = [0]

            def link(ins):
                steps[0] += 1
                ins.then_inc(dve_step, 1)
                dve.wait_ge(dve_step, steps[0])

            def split_lo(c):
                dve.wait_ge(hi_ready, c + 1)
                nc.vector.tensor_tensor(w_lo[:, slot_of(c), :], w_raw[:, c % RAW, :],
                                        w_hi[:, slot_of(c), :].bitcast(F32), ALU.subtract).then_inc(lo_ready, 1)

            def turn_lo(e, t, banks):
                for b, bank in enumerate(banks):
                    dve.wait_ge(hT_hi_set, 2 * e + b + 1)
                    part = (slice(None), slice(4 * b, 4 * b + 4), slice(t * P, (t + 1) * P))
                    nc.vector.tensor_tensor(hT_lo[part], bank.rearrange("p (k n) -> p k n", k=4),
                                            hT_hi[part].bitcast(F32), ALU.subtract).then_inc(hT_lo_set, 1)

            def conv(c):
                b, h = divmod(c, 2)
                dve.wait_ge(tap3_done, c + 1)
                for s in range(1, CONV):
                    for f in range(2):
                        ft = 4 * b + 2 * h + f
                        col = 4 + (CONV - 1 - s) * 8 + ft
                        n = 6 * c + 2 * (s - 1) + f
                        if s > 1:
                            dve.wait_ge(conv_step, n - 1)
                        ins = nc.vector.scalar_tensor_tensor(
                            out=qk_m[:, ft, s:S], in0=pp[:, 2 * (b % 2) + h, f * S:(f + 1) * S - s],
                            scalar=vcol[:, col:col + 1], in1=qk_m[:, ft, s:S], op0=ALU.mult, op1=ALU.add)
                        ins.then_inc(conv_step, 1)

            def score_w(h):
                dve.wait_ge(qk_m_done, h + 1)
                if h == 0:
                    dve.wait_ge(w_masked, 2)
                nc.vector.scalar_tensor_tensor(out=wm[:, h, :], in0=pa[:, h % 2, 0:384], scalar=D_M ** -0.5,
                                               in1=wm[:, h, :], op0=ALU.mult, op1=ALU.mult).then_inc(w_ready, 1)

            def score_max(p):
                dve.wait_ge(alibi_set, 2)
                if p >= 2:
                    dve.wait_ge(prob_turned, p - 1)
                for e in range(2):
                    dve.wait_ge(scores_done, 2 * p + e + 1)
                    for lo, hi, q in ((0, 128, 0), (128, 384, 1)):
                        n = 4 * p + 2 * e + q
                        ins = nc.vector.tensor_tensor_reduce(
                            out=prob[:, p % 2, e, lo:hi], in0=pa[:, 2 + e, lo:hi],
                            in1=alibi[:, 2 * p + e, lo:hi], scale=1.0, scalar=LOWEST, op0=ALU.add,
                            op1=ALU.max, accum_out=smax[:, n:n + 1])
                    ins.then_inc(scores_read, 1)
                dve.wait_ge(scores_read, 2 * p + 2)
                nc.vector.tensor_scalar(nsmax[:, 4 * p:4 * p + 4], smax[:, 4 * p:4 * p + 4], -D_A ** -0.5, None,
                                        ALU.mult).then_inc(nsmax_set, 1)

            def prob_scale(p):
                dve.wait_ge(exp_done, p + 1)
                link(nc.vector.reciprocal(sinv[:, 4 * p:4 * p + 4], ssum[:, 4 * p:4 * p + 4]))
                for e in range(2):
                    for lo, hi, q in ((0, 128, 0), (128, 384, 1)):
                        n = 4 * p + 2 * e + q
                        part = prob[:, p % 2, e, lo:hi]
                        ins = nc.vector.tensor_scalar(part, part, sinv[:, n:n + 1], None, ALU.mult)
                ins.then_inc(prob_ready, 1)

            def ya_lo(p):
                dve.wait_ge(ya_hi_set, p + 1)
                nc.vector.tensor_tensor(yT_lo[:, p, :], pa[:, 0, 0:S], yT_hi[:, p, :].bitcast(F32),
                                        ALU.subtract).then_inc(ya_lo_set, 1)

            def head_out(h):
                dve.wait_ge(num_done, h + 1)
                if h == 0:
                    dve.wait_ge(proj_free[0], 6)
                both = pa[:, 1, 0:2 * (D_M + 1)].rearrange("p (t n) -> p t n", t=T)
                link(nc.vector.scalar_tensor_tensor(
                    out=den[:, 2 * h:2 * h + 2], in0=both[:, :, D_M], scalar=-1.0,
                    in1=rcol[:, 8:16].rearrange("p (t h) -> p t h", t=T)[:, :, h], op0=ALU.mult, op1=ALU.max))
                link(nc.vector.tensor_tensor(den[:, 2 * h:2 * h + 2], both[:, :, D_M], den[:, 2 * h:2 * h + 2],
                                             ALU.max))
                link(nc.vector.reciprocal(dinv[:, 2 * h:2 * h + 2], den[:, 2 * h:2 * h + 2]))
                for t in range(T):
                    part = o_t[:, t, h * D_M:(h + 1) * D_M]
                    ins = nc.vector.scalar_tensor_tensor(
                        out=part, in0=both[:, t, 0:D_M], scalar=dinv[:, 2 * h + t:2 * h + t + 1], in1=part,
                        op0=ALU.mult, op1=ALU.mult)
                ins.then_inc(num_read, 1)
                dve.wait_ge(num_read, h + 1)
                for t in range(T):
                    ins = nc.vector.bn_stats(bn[:, 2 * h + t, :], o_t[:, t, h * D_M:(h + 1) * D_M])
                link(ins)
                for t in range(T):
                    ins = nc.vector.bn_aggr(mv[:, 2 * h + t, :], bn[:, 2 * h + t, :])
                ins.then_inc(var_set, 1)

            def merge(t, banks):
                dve.wait_ge(proj_free[0], 10)
                dve.wait_ge(proj_free[1], 8)
                if t == 0:
                    dve.wait_ge(wout_done, 1)
                else:
                    dve.wait_ge(chunk_used, C_OUT + 2)
                nc.vector.tensor_tensor(ra_t[:, t], banks[:, 0:2, :].rearrange("p b n -> p (b n)"), ra_t[:, t],
                                        ALU.mult)
                if t == 0:
                    dve.wait_ge(wout_done, 2)
                else:
                    dve.wait_ge(chunk_used, C_OUT + 4)
                link(nc.vector.tensor_tensor(rb_t[:, t], banks[:, 2:4, :].rearrange("p b n -> p (b n)"),
                                             rb_t[:, t], ALU.mult))
                nc.vector.tensor_tensor(ra_t[:, t], ra_t[:, t], rb_t[:, t], ALU.add).then_inc(merged, 1)

            def residual(t, banks, done, value, ready):
                dve.wait_ge(done, value)
                nc.vector.tensor_tensor(x_t[:, t], banks.rearrange("p b n -> p (b n)"), x_t[:, t],
                                        ALU.add).then_inc(ready, 1)

            def norm(n, t, gain, ready):
                dve.wait_ge(rstd_done, n + 1)
                nc.vector.scalar_tensor_tensor(out=rb_t[:, t], in0=x_t[:, t], scalar=rstd[:, n:n + 1], in1=gain,
                                               op0=ALU.mult, op1=ALU.mult).then_inc(ready, 1)

            dve.wait_ge(gmix_spread, 1)
            gain_mix = pa[:, 2:4, :].rearrange("p b n -> p (b n)")
            norm(0, 0, gain_mix, normed)
            norm(1, 1, gain_mix, normed)
            turn_lo(0, 0, (pa[:, 0, :], pa[:, 1, :]))
            split_lo(0)
            turn_lo(1, 1, (pp[:, 2, :], pp[:, 3, :]))
            dve.wait_ge(vec_turned, 1)
            nc.vector.tensor_copy(vcol[:, :], pp[:, 1, 0:36]).then_inc(vcol_set, 1)
            for c in range(1, AHEAD):
                split_lo(c)
                if c == 2:
                    dve.wait_ge(wif_loaded, 16)
                    dve.wait_ge(wif_zeroed, 1)
                    nc.vector.tensor_copy(wif_pad[:, :, 0:4], wif_raw[:, :, 0:4]).then_inc(wif_padded, 1)
                    nc.vector.tensor_copy(wif_pad[:, :, 32:36], wif_raw[:, :, 4:8]).then_inc(wif_padded, 1)
            dve.wait_ge(wif_hi_set, 1)
            nc.vector.tensor_tensor(wif_lo[:, :, :], wif_pad, wif_hi[:, :, :].bitcast(F32), ALU.subtract
                                    ).then_inc(wif_lo_set, 1)

            for c in range(C_OUT):
                split_lo(c + AHEAD)
                if c == 2:
                    dve.wait_ge(gates_done, 1)
                    dve.wait_ge(bif_loaded, 32)
                    nc.vector.tensor_scalar(row_i, pa[0:H_M, 0, 0:S], b_if[:, 0:1], None, ALU.add)
                    link(nc.vector.tensor_scalar(row_f, pa[32:32 + H_M, 0, 0:S], b_if[:, 1:2], None, ALU.add))
                    nc.vector.scalar_tensor_tensor(out=row_l, in0=row_f, scalar=-1.0, in1=row_f, op0=ALU.mult,
                                                   op1=ALU.min).then_inc(gate_rows_set, 1)
                if c == 3:
                    dve.wait_ge(log_done, 1)
                    dve.wait_ge(ones_set, 2)
                    link(nc.vector.scalar_tensor_tensor(out=row_f, in0=row_f, scalar=0.0, in1=row_l,
                                                        op0=ALU.min, op1=ALU.subtract))
                    link(nc.vector.tensor_tensor_scan(row_b, row_one, row_f, 0.0, ALU.mult, ALU.add))
                    link(nc.vector.tensor_tensor(row_i, row_i, row_b, ALU.subtract))
                    link(nc.vector.tensor_tensor_scan(row_m, row_one, row_i, 0.0, ALU.mult, ALU.max))
                    nc.vector.tensor_tensor(row_e, row_b, row_m, ALU.add).then_inc(scans_done, 1)
                if c == 6:
                    dve.wait_ge(cols_turned, 1)
                    nc.vector.tensor_copy(rcol[:, :], pa[:, 1, 0:16]).then_inc(rcol_set, 1)
                if c == 8:
                    score_w(0)
                    score_w(1)
                if c == 9:
                    score_w(2)
                    score_w(3)
                if c == 10:
                    score_max(0)
                if c == 11:
                    prob_scale(0)
                    score_max(1)
                if c == 12:
                    prob_scale(1)
                    dve.wait_ge(cols_turned, 1)
                    dve.wait_ge(m_spread, 1)
                    nc.vector.memset(vm[:, :, :, D_M:D_M + 1], 1.0).then_inc(v_ml_set, 1)
                    for t in range(T):
                        if t == 0:
                            dve.wait_ge(tile0_done, 2)
                        else:
                            dve.wait_ge(chunk_used, 2 * 5 + 2)
                        nc.vector.tensor_copy(vm[:, t, :, 0:D_M],
                                              pp[:, 2 + t, :].rearrange("p (h n) -> p h n", h=H_M)
                                              ).then_inc(proj_free[1], 1)
                if c == 13:
                    ya_lo(0)
                    score_max(2)
                if c == 14:
                    prob_scale(2)
                if c == 15:
                    ya_lo(1)
                    score_max(3)
                if c == 16:
                    prob_scale(3)
                    head_out(0)
                if c == 17:
                    ya_lo(2)
                    head_out(1)
                if c == 18:
                    ya_lo(3)
                    head_out(2)
                if c == 19:
                    head_out(3)
                    dve.wait_ge(lnr_set, 1)
                    dve.wait_ge(var_set, H_M)
                    for h in range(H_M):
                        for t in range(T):
                            part = o_t[:, t, h * D_M:(h + 1) * D_M]
                            n = 2 * h + t
                            ins = nc.vector.tensor_scalar(part, part, mv[:, n, 0:1], lnr[:, n:n + 1],
                                                          ALU.subtract, ALU.mult)
                    ins.then_inc(y_normed, 1)
                if c < 4:
                    conv(c)
                if c == 21:
                    for b in range(2):
                        dve.wait_ge(ym_hi_set, b + 1)
                        for f in range(2):
                            h = 2 * b + f
                            ins = nc.vector.scalar_tensor_tensor(
                                out=yT_lo[:, 4 + h, :], in0=pa[:, 2 + b, f * S:(f + 1) * S],
                                scalar=vcol[:, h:h + 1], in1=yT_hi[:, 4 + h, :].bitcast(F32),
                                op0=ALU.mult, op1=ALU.subtract)
                        ins.then_inc(ym_lo_set, 1)
            for c in range(C_OUT + AHEAD, C_OUT + 6):
                split_lo(c)
            merge(0, pa)
            for c in range(C_OUT + 6, C_OUT + 8):
                split_lo(c)
            turn_lo(2, 0, (pa[:, 0, :], pa[:, 1, :]))
            merge(1, pp)
            for c in range(C_OUT + 8, C_FFN + 2):
                split_lo(c)
            turn_lo(3, 1, (pp[:, 0, :], pp[:, 1, :]))
            dve.wait_ge(x_reloaded, 16)
            residual(0, pa[:, 2:4, :], wo_done, 1, x2_ready)
            dve.wait_ge(gain_ffn_loaded, 16)
            norm(2, 0, gain_ffn, normed)
            turn_lo(4, 0, (pa[:, 0, :], pa[:, 1, :]))
            residual(1, pp[:, 2:4, :], chunk_used, C_WO + 4, x2_ready)
            norm(3, 1, gain_ffn, normed)
            turn_lo(5, 1, (pp[:, 0, :], pp[:, 1, :]))

            def hidden(i, g):
                dve.wait_ge(silu_f_done, i * 2 + g + 1)
                dve.wait_ge(chunk_used, i * 6 + (C_FFN + max(3 * g + 1, 2)))
                nc.vector.tensor_tensor(hid[:, g % 2, :], pa[:, 2 + g % 2, :], hid[:, g % 2, :], ALU.mult
                                        ).then_inc(prod_done, 1)
                dve.wait_ge(a_hi_set, i * 2 + g + 1)
                if g >= 2 or i is not FIRST:
                    dve.wait_ge(chunk_used, i * 6 + (C_FFN + 3 * g - 1))
                part = (slice(None), slice(2 * (g % 2), 2 * (g % 2) + 2), slice(None))
                nc.vector.tensor_tensor(yT_lo[part], hid[:, g % 2, :].rearrange("p (f n) -> p f n", f=2),
                                        yT_hi[part].bitcast(F32), ALU.subtract).then_inc(a_lo_set, 1)

            def two_groups(i):
                for j in range(2):
                    c = C_FFN + 2 + 3 * j
                    for r in range(3):
                        dve.wait_ge(hi_ready, i * 6 + (c + r + 1))
                        nc.vector.tensor_tensor(w_lo[:, slot_of(c + r), :], w_raw[:, (c + r) % RAW, :],
                                                w_hi[:, slot_of(c + r), :].bitcast(F32), ALU.subtract
                                                ).then_inc(lo_ready, 1)
                    hidden(i, 1 + j)

            hidden(FIRST, 0)
            two_groups(FIRST)
            with dve.Fori(1, (FG - 1) // 2) as i:
                two_groups(i)
            split_lo(C_FFN + 2 + 3 * (FG - 1))
            dve.wait_ge(gain_fin_loaded, 16)
            residual(0, pp[:, 0:2, :], ffn_out_done, 1, x3_ready)
            residual(1, pp[:, 2:4, :], ffn_out_done, 2, x3_ready)
            norm(4, 0, gain_fin, out_ready)
            norm(5, 1, gain_fin, out_ready)

        @block.tensor
        def _(pe):
            mm = nc.tensor.matmul

            def feature_chunk(c, bank):
                s = slot_of(c)
                hi, lo = w_hi[:, s, :], w_lo[:, s, :]
                for f in range(2):
                    o = bank[:, f * S:(f + 1) * S]
                    for k in range(KT):
                        w = slice(k * 256 + f * P, k * 256 + (f + 1) * P)
                        mm(o, hi[:, w], hT_hi[:, k, :], start=(k == 0), stop=False)
                        mm(o, hi[:, w], hT_lo[:, k, :], start=False, stop=False)
                        ins = mm(o, lo[:, w], hT_hi[:, k, :], start=False, stop=(k == KT - 1))
                return ins

            def token_product(o, aT_hi, aT_lo, k, t, w, s, start, stop):
                tok = slice(t * P, (t + 1) * P)
                mm(o, aT_hi[:, k, tok], w_hi[:, s, w], start=start, stop=False)
                mm(o, aT_lo[:, k, tok], w_hi[:, s, w], start=False, stop=False)
                return mm(o, aT_hi[:, k, tok], w_lo[:, s, w], start=False, stop=stop)

            def turn(src, banks):
                for b, bank in enumerate(banks):
                    for k in range(4):
                        n = 4 * b + k
                        ins = nc.tensor.transpose(bank[:, k * P:(k + 1) * P], src[:, n * P:(n + 1) * P], ident[:, :])
                    ins.then_inc(turned, 1)

            pe.wait_ge(ones_set, 1)
            pe.wait_ge(gmix_loaded, 16)
            for n in range(2):
                ins = mm(pa[:, 2 + n, :], ones_row, gmix_row[:, 512 * n:512 * (n + 1)], start=True, stop=True)
            ins.then_inc(gmix_spread, 1)
            pe.wait_ge(ident_set, 1)
            pe.wait_ge(vec_loaded, 32)
            nc.tensor.transpose(pp[:, 1, 0:36], vec_rows, ident[0:36, 0:36]).then_inc(vec_turned, 1)
            pe.wait_ge(normed, 1)
            turn(rb_t[:, 0], (pa[:, 0, :], pa[:, 1, :]))
            pe.wait_ge(normed, 2)
            turn(rb_t[:, 1], (pp[:, 2, :], pp[:, 3, :]))
            pe.wait_ge(hT_lo_set, 4)

            def gates():
                pe.wait_ge(wif_lo_set, 1)
                for k in range(KT):
                    mm(pa[0:36, 0, 0:S], wif_hi[:, k, :], hT_hi[:, k, :], start=(k == 0), stop=False)
                    mm(pa[0:36, 0, 0:S], wif_hi[:, k, :], hT_lo[:, k, :], start=False, stop=False)
                    ins = mm(pa[0:36, 0, 0:S], wif_lo[:, k, :], hT_hi[:, k, :], start=False, stop=(k == KT - 1))
                ins.then_inc(gates_done, 1)

            def gate_columns():
                pe.wait_ge(scans_done, 1)
                pe.wait_ge(sel_set, 1)
                for h in range(H_M):
                    ins = mm(pa[:, 2 + h // 2, (h % 2) * S:(h % 2 + 1) * S], sel[:, h * P:(h + 1) * P], row_m,
                             start=True, stop=True)
                ins.then_inc(m_spread, 1)
                pe.wait_ge(exp_m_done, 1)
                for n, row in enumerate((row_i, row_e)):
                    for t in range(T):
                        ins = nc.tensor.transpose(pa[:, 1, 8 * n + 4 * t:8 * n + 4 * t + 4],
                                                  row[:, t * P:(t + 1) * P], ident[0:H_M, 0:H_M])
                ins.then_inc(cols_turned, 1)

            def mlstm_scores(h):
                if h == 0:
                    pe.wait_ge(silu_done, 4)
                    pe.wait_ge(rcol_set, 1)
                if h >= 2:
                    pe.wait_ge(w_ready, h - 1)
                q, k = qk_m[:, h, :], qk_m[:, H_M + h, :]
                mm(pa[:, h % 2, 0:S], k[:, 0:P], q, start=True, stop=True)
                mm(pa[:, h % 2, S:384], k[:, P:S], q[:, P:S], start=True, stop=True).then_inc(qk_m_done, 1)

            def scores(p):
                if p == 0:
                    pe.wait_ge(w_exp_done, 2 * H_M)
                    pe.wait_ge(proj_free[0], 2)
                    pe.wait_ge(proj_free[1], 2)
                if p == 1:
                    pe.wait_ge(scores_read, 2)
                if p >= 2:
                    pe.wait_ge(pT_set, p - 1)
                for e in range(2):
                    half = slice(e * D_A, (e + 1) * D_A)
                    q, k = qk_a[half, p, :], qk_a[half, 4 + p, :]
                    mm(pa[:, 2 + e, 0:P], q[:, 0:P], k[:, 0:P], start=True, stop=True)
                    mm(pa[:, 2 + e, P:384], q[:, P:S], k, start=True, stop=True).then_inc(scores_done, 1)

            def prob_turn(p):
                pe.wait_ge(prob_ready, p + 1)
                pe.wait_ge(scores_read, min(2 * p + 4, H_A))
                if p == 3:
                    pe.wait_ge(pT_set, 3)
                for e in range(2):
                    for n in range(3):
                        ins = nc.tensor.transpose(pa[:, 2 + e, n * P:(n + 1) * P],
                                                  prob[:, p % 2, e, n * P:(n + 1) * P], ident[:, :])
                ins.then_inc(prob_turned, 1)

            def pv(p):
                pe.wait_ge(pT_set, p + 1)
                if p:
                    pe.wait_ge(ya_lo_set, p)
                else:
                    pe.wait_ge(w_ready, H_M)
                    pe.wait_ge(proj_free[0], 4)
                for e in range(2):
                    half = slice(e * D_A, (e + 1) * D_A)
                    cols = slice((2 * p + e) * D_A, (2 * p + e + 1) * D_A)
                    mm(pa[half, 0, 0:S], va[:, 0, cols], pT[:, e, 0:S], start=True, stop=False)
                    ins = mm(pa[half, 0, P:S], va[:, 1, cols], pT[:, e, S:384], start=False, stop=True)
                ins.then_inc(pv_done, 1)

            def numerators(h):
                if h == 0:
                    pe.wait_ge(w_ready, H_M)
                    pe.wait_ge(v_ml_set, 1)
                    pe.wait_ge(proj_free[1], 4)
                else:
                    pe.wait_ge(num_read, h)
                n = D_M + 1
                mm(pa[:, 1, 0:n], wm[:, h, 0:P], vm[:, 0, h, :], start=True, stop=True)
                mm(pa[:, 1, n:2 * n], wm[:, h, P:S], vm[:, 0, h, :], start=True, stop=False)
                mm(pa[:, 1, n:2 * n], wm[:, h, S:384], vm[:, 1, h, :], start=False, stop=True).then_inc(num_done, 1)

            def ym_turn():
                pe.wait_ge(y_normed, 1)
                pe.wait_ge(pT_set, 4)
                for b in range(2):
                    for f in range(2):
                        for t in range(T):
                            h = 2 * b + f
                            ins = nc.tensor.transpose(pa[:, 2 + b, f * S + t * P:f * S + (t + 1) * P],
                                                      o_t[:, t, h * D_M:(h + 1) * D_M], ident[:, :])
                    ins.then_inc(ym_turned, 1)

            for c in range(C_OUT):
                b, h = divmod(c, 2)
                pe.wait_ge(lo_ready, c + 1)
                if b < FEATURE_MAJOR:
                    if b >= 2:
                        pe.wait_ge(conv_step, 6 * (c - 3))
                    if c == 1:
                        pe.wait_ge(vcol_set, 1)
                    feature_chunk(c, pp[:, 2 * (b % 2) + h, :]).then_inc(chunk_used, 1)
                else:
                    for t in range(T):
                        if h == 0:
                            pe.wait_ge(proj_free[b % 2], 2 * (b // 2 - 1) - 1 + t)
                        for k in range(4):
                            ins = token_product(pp[:, 2 * (b % 2) + t, :], hT_hi, hT_lo, 4 * h + k, t,
                                                slice(512 * k, 512 * (k + 1)), slot_of(c),
                                                h == 0 and k == 0, h == 1 and k == 3)
                        if h == 1 and t == 0:
                            ins.then_inc(tile0_done, 1)
                    ins.then_inc(chunk_used, 1)
                if c == 1:
                    gates()
                elif c == 5:
                    gate_columns()
                elif c == 7:
                    mlstm_scores(0)
                    mlstm_scores(1)
                elif c == 8:
                    mlstm_scores(2)
                    mlstm_scores(3)
                elif c in (9, 10):
                    scores(c - 9)
                elif c == 11:
                    prob_turn(0)
                elif c == 12:
                    pv(0)
                    scores(2)
                elif c == 13:
                    prob_turn(1)
                elif c == 14:
                    pv(1)
                    scores(3)
                elif c == 15:
                    prob_turn(2)
                    numerators(0)
                elif c == 16:
                    pv(2)
                    prob_turn(3)
                    numerators(1)
                elif c == 17:
                    pv(3)
                    numerators(2)
                elif c == 18:
                    numerators(3)
                elif c == 19:
                    ym_turn()

            for t in range(T):
                banks = (pa, pp)[t]
                if t == 1:
                    pe.wait_ge(proj_free[0], 10)
                    pe.wait_ge(proj_free[1], 8)
                for m in range(2):
                    if t == 0:
                        if m == 0:
                            pe.wait_ge(ya_lo_set, 4)
                            pe.wait_ge(num_read, H_M)
                        else:
                            pe.wait_ge(ym_lo_set, 2)
                    for n in range(2):
                        c = C_OUT + 2 * m + n
                        pe.wait_ge(lo_ready, c + 1)
                        for k in range(4):
                            ins = token_product(banks[:, 2 * m + n, :], yT_hi, yT_lo, 4 * m + k, t,
                                                slice(512 * k, 512 * (k + 1)), slot_of(c), k == 0, k == 3)
                        if t == 1:
                            ins.then_inc(chunk_used, 1)
                    if t == 0:
                        ins.then_inc(wout_done, 1)

            def out_product(t, banks):
                for n in range(2):
                    for h in range(2):
                        c = C_WO + 2 * n + h
                        pe.wait_ge(lo_ready, c + 1)
                        for k in range(4):
                            ins = token_product(banks[:, n, :], hT_hi, hT_lo, 4 * h + k, t,
                                                slice(512 * k, 512 * (k + 1)), slot_of(c),
                                                h == 0 and k == 0, h == 1 and k == 3)
                        if t == 1:
                            ins.then_inc(chunk_used, 1)
                if t == 0:
                    ins.then_inc(wo_done, 1)

            pe.wait_ge(merged, 1)
            turn(ra_t[:, 0], (pa[:, 0, :], pa[:, 1, :]))
            pe.wait_ge(hT_lo_set, 6)
            out_product(0, pa[:, 2:4, :])
            pe.wait_ge(merged, 2)
            turn(ra_t[:, 1], (pp[:, 0, :], pp[:, 1, :]))
            pe.wait_ge(hT_lo_set, 8)
            out_product(1, pp[:, 2:4, :])

            def first_group(t):
                tok = slice(t * P, (t + 1) * P)
                for r in range(2):
                    s = slot_of(C_FFN + r)
                    pe.wait_ge(lo_ready, C_FFN + r + 1)
                    for f in range(2):
                        o = pa[:, 2 * r, f * S + t * P:f * S + (t + 1) * P]
                        for k in range(KT):
                            w = slice(k * 256 + f * P, k * 256 + (f + 1) * P)
                            mm(o, w_hi[:, s, w], hT_hi[:, k, tok], start=(k == 0), stop=False)
                            mm(o, w_hi[:, s, w], hT_lo[:, k, tok], start=False, stop=False)
                            ins = mm(o, w_lo[:, s, w], hT_hi[:, k, tok], start=False, stop=(k == KT - 1))
                    if t == 1:
                        ins.then_inc(chunk_used, 1)

            pe.wait_ge(normed, 3)
            turn(rb_t[:, 0], (pa[:, 0, :], pa[:, 1, :]))
            pe.wait_ge(hT_lo_set, 10)
            first_group(0)
            pe.wait_ge(normed, 4)
            turn(rb_t[:, 1], (pp[:, 0, :], pp[:, 1, :]))
            pe.wait_ge(hT_lo_set, 12)
            first_group(1)

            def down(a, s, t, k, start, stop):
                for n in range(2):
                    ins = token_product(pp[:, 2 * t + n, :], yT_hi, yT_lo, 2 * a + k, t,
                                        slice(1024 * k + 512 * n, 1024 * k + 512 * (n + 1)), s, start, stop)
                return ins

            def group(i, g):
                start = i is FIRST and g == 1
                c = C_FFN + 3 * g - 1
                for r in range(2):
                    pe.wait_ge(lo_ready, i * 6 + (c + r + 1))
                    if not start:
                        pe.wait_ge((silu_f_done, prod_done)[r], i * 2 + (g - 1))
                    feature_chunk(c + r, pa[:, 2 * r + g % 2, :]).then_inc(chunk_used, 1)
                pe.wait_ge(lo_ready, i * 6 + (c + 3))
                pe.wait_ge(a_lo_set, i * 2 + g)
                for t in range(T):
                    for k in range(2):
                        ins = down((g - 1) % 2, slot_of(c + 2), t, k, start and k == 0, False)
                ins.then_inc(chunk_used, 1)

            group(FIRST, 1)
            group(FIRST, 2)
            with pe.Fori(1, (FG - 1) // 2) as i:
                group(i, 1)
                group(i, 2)
            c = C_FFN + 2 + 3 * (FG - 1)
            pe.wait_ge(lo_ready, c + 1)
            pe.wait_ge(a_lo_set, FG)
            for t in range(T):
                for k in range(2):
                    ins = down((FG - 1) % 2, slot_of(c), t, k, False, k == 1)
                ins.then_inc(ffn_out_done, 1)


_INS = ['x', 'mix_norm_g', 'w_in', 'conv_qk', 'b_igate', 'b_fgate', 'mlstm_norm_g', 'w_out_attn',
        'w_out_mlstm', 'w_o', 'ffn_norm_g', 'w_ffn_gate', 'w_ffn_up', 'w_ffn_down', 'final_norm_g']


def kernel(**inputs):
    import numpy as np
    import concourse.bacc as bacc
    from concourse.bass_utils import run_bass_kernel_spmd

    nc = bacc.Bacc("TRN2", target_bir_lowering=False, num_devices=1)
    arrays, args = {}, []
    for name in _INS:
        a = np.ascontiguousarray(inputs[name])
        arrays[f"in_{name}"] = a
        args.append(nc.dram_tensor(f"in_{name}", a.shape, mybir.dt.from_np(a.dtype), kind="ExternalInput").ap())
    args.append(nc.dram_tensor("out_x", (1, S, D), F32, kind="ExternalOutput").ap())
    build(nc, *args)
    return run_bass_kernel_spmd(nc, [arrays], core_ids=[0]).results[0]["out_x"]
```

```python
from contextlib import ExitStack

import concourse.bass as bass
from concourse import mybir

ALU = mybir.AluOpType
ACT = mybir.ActivationFunctionType
F32 = mybir.dt.float32
F32R = mybir.dt.float32r
BF16 = mybir.dt.bfloat16

P = 128
S = 256
T = S // P
D = 1024
KT = D // P
H_A, D_A = 8, 64
H_M, D_M = 4, 128
W_A, W_M = H_A * D_A, H_M * D_M
CONV = 4
F = 2816
EPS = 1e-6
MASKED = -1e30
LOWEST = -3.0e38

Q_A, K_A, V_A = 0, W_A, 2 * W_A
Q_M = 3 * W_A
K_M, V_M, O_M = Q_M + W_M, Q_M + 2 * W_M, Q_M + 3 * W_M
I_M = Q_M + 4 * W_M
G_A = I_M + 2 * H_M
G_M = G_A + D

CH = 2048
RAW = 3
RING = 6
BLOCKS = [Q_M, K_M, Q_A, K_A, V_A, V_M, O_M, G_A, G_A + 512, G_M, G_M + 512]
FEATURE_MAJOR = 4
NB = len(BLOCKS)
C_OUT = 2 * NB
C_WO = C_OUT + 4
C_FFN = C_WO + 4
FG = F // 256
FIRST = 0
WARM_A, WARM_B = 20, 10
AHEAD = 4


def slot_of(c):
    return c % RING


def build(nc, x, mix_norm_g, w_in, conv_qk, b_igate, b_fgate, mlstm_norm_g, w_out_attn,
          w_out_mlstm, w_o, ffn_norm_g, w_ffn_gate, w_ffn_up, w_ffn_down, final_norm_g, out):
    x_d = x[0].rearrange("(t p) n -> p t n", p=P)
    out_d = out[0].rearrange("(t p) n -> p t n", p=P)
    w_in_k = w_in[0].rearrange("(k p) n -> p k n", p=P)
    wo_k = w_o[0].rearrange("(k p) n -> p k n", p=P)
    woa_k = w_out_attn[0].rearrange("(k p) n -> p k n", p=P)
    wom_k = w_out_mlstm[0].rearrange("(k p) n -> p k n", p=P)
    gate_k = w_ffn_gate[0].rearrange("(k p) n -> p k n", p=P)
    up_k = w_ffn_up[0].rearrange("(k p) n -> p k n", p=P)
    down_k = w_ffn_down[0].rearrange("(k p) n -> p k n", p=P)

    with ExitStack() as ctx:
        def sb(name, shape, dt=F32):
            return ctx.enter_context(nc.sbuf_tensor(name, shape, dt))

        def sem(name):
            return ctx.enter_context(nc.semaphore(name))

        w_raw = sb("w_raw", [P, RAW, CH])
        w_hi = sb("w_hi", [P, RING, CH], F32R)
        w_lo = sb("w_lo", [P, RING, CH], F32R)
        hT_hi = sb("hT_hi", [P, KT, S], F32R)
        hT_lo = sb("hT_lo", [P, KT, S], F32R)
        yT_hi = sb("yT_hi", [P, 8, S], F32R)
        yT_lo = sb("yT_lo", [P, 8, S], F32R)
        wif_hi = sb("wif_hi", [P, KT, 36], F32R)
        wif_lo = sb("wif_lo", [P, KT, 36], F32R)
        x_sb = sb("x_sb", [P, T * D])
        region_a = sb("region_a", [P, T * D])
        region_b = sb("region_b", [P, T * D])
        v_att = sb("v_att", [P, T * W_A])
        v_ml = sb("v_ml", [P, T * H_M * (D_M + 1)])
        o_sb = sb("o_sb", [P, T * W_M])
        w_ml = sb("w_ml", [P, H_M * 384])
        pT = sb("pT", [P, 2, 384])
        alibi = sb("alibi", [P, H_A, 384], BF16)
        ident = sb("ident", [P, P])
        vcol = sb("vcol", [P, 36])
        sumsq = sb("sumsq", [P, 12])
        meansq = sb("meansq", [P, 6])
        rstd = sb("rstd", [P, 6])
        minus_half = sb("minus_half", [P, 8])
        b_if = sb("b_if", [H_M, 2])
        rcol = sb("rcol", [P, 16])
        smax = sb("smax", [P, 16])
        nsmax = sb("nsmax", [P, 16])
        ssum = sb("ssum", [P, 16])
        sinv = sb("sinv", [P, 16])
        den = sb("den", [P, 8])
        dinv = sb("dinv", [P, 8])
        bn = sb("bn", [P, 8, 6])
        mv = sb("mv", [P, 8, 2])
        lnv = sb("lnv", [P, 8])
        lnr = sb("lnr", [P, 8])

        x_t = x_sb[:, :].rearrange("p (t n) -> p t n", t=T)
        prob = x_sb[:, 0:1536].rearrange("p (s e n) -> p s e n", s=2, e=2)
        ra_t = region_a[:, :].rearrange("p (t n) -> p t n", t=T)
        rb_t = region_b[:, :].rearrange("p (t n) -> p t n", t=T)
        qk_m = region_a[:, :].rearrange("p (f n) -> p f n", f=8)
        qk_a = region_b[:, :].rearrange("p (f n) -> p f n", f=8)
        hid = region_a[:, 0:1024].rearrange("p (s n) -> p s n", s=2)
        va = v_att[:, :].rearrange("p (t n) -> p t n", t=T)
        vm = v_ml[:, :].rearrange("p (t h n) -> p t h n", t=T, h=H_M)
        o_t = o_sb[:, :].rearrange("p (t n) -> p t n", t=T)
        wm = w_ml[:, :].rearrange("p (h n) -> p h n", h=H_M)
        gain_ffn = v_att[:, 0:D]
        gain_fin = v_ml[:, 0:D]
        gmix_row = v_ml[0:1, 0:D]
        vec_rows = pT[0:36, 1, 128:256]
        row_i, row_f, row_l, row_b = (o_sb[0:H_M, n * S:(n + 1) * S] for n in range(4))
        row_m, row_e = (v_ml[0:H_M, n * S:(n + 1) * S] for n in range(2))
        row_one = w_ml[0:H_M, 0:S]
        ones_row = w_ml[0:1, 256:384]
        wif_pad = w_ml[:, 512:512 + KT * 36].rearrange("p (k n) -> p k n", k=KT)
        wif_raw = w_ml[:, 1024:1024 + KT * 8].rearrange("p (k n) -> p k n", k=KT)
        dist = w_ml[:, 1100:1100 + 384]
        sel = pT[0:H_M, :, :].rearrange("p e n -> p (e n)")[:, 0:512]

        pp = ctx.enter_context(nc.psum_tensor("pp", [P, 4, 512], F32))
        pa = ctx.enter_context(nc.psum_tensor("pa", [P, 4, 512], F32))

        x_loaded = [sem(f"x_loaded{t}") for t in range(T)]
        gmix_loaded = sem("gmix_loaded")
        vec_loaded = sem("vec_loaded")
        wif_loaded = sem("wif_loaded")
        bif_loaded = sem("bif_loaded")
        gain_ffn_loaded = sem("gain_ffn_loaded")
        gain_fin_loaded = sem("gain_fin_loaded")
        x_reloaded = sem("x_reloaded")
        chunk_loaded = [sem(f"chunk_loaded{s}") for s in range(RAW)]
        hi_ready = sem("hi_ready")
        lo_ready = sem("lo_ready")
        chunk_used = sem("chunk_used")
        ones_set = sem("ones_set")
        pool_step = sem("pool_step")
        ident_set = sem("ident_set")
        wif_zeroed = sem("wif_zeroed")
        sel_set = sem("sel_set")
        alibi_set = sem("alibi_set")
        sumsq_done = sem("sumsq_done")
        rstd_done = sem("rstd_done")
        normed = sem("normed")
        squares_warm = sem("squares_warm")
        first_half_loaded = sem("first_half_loaded")
        first_half_hi = sem("first_half_hi")
        first_half_lo = sem("first_half_lo")
        gmix_spread = sem("gmix_spread")
        vec_turned = sem("vec_turned")
        vcol_set = sem("vcol_set")
        turned = sem("turned")
        hT_hi_set = sem("hT_hi_set")
        hT_lo_set = sem("hT_lo_set")
        wif_hi_set = sem("wif_hi_set")
        wif_lo_set = sem("wif_lo_set")
        wif_padded = sem("wif_padded")
        tile0_done = sem("tile0_done")
        proj_free = [sem(f"proj_free{s}") for s in range(2)]
        tap3_done = sem("tap3_done")
        conv_step = sem("conv_step")
        silu_done = sem("silu_done")
        gates_done = sem("gates_done")
        gate_rows_set = sem("gate_rows_set")
        log_done = sem("log_done")
        exp1_done = sem("exp1_done")
        scans_done = sem("scans_done")
        exp_m_done = sem("exp_m_done")
        cols_turned = sem("cols_turned")
        m_spread = sem("m_spread")
        rcol_set = sem("rcol_set")
        w_exp_done = sem("w_exp_done")
        w_masked = sem("w_masked")
        qk_m_done = sem("qk_m_done")
        w_ready = sem("w_ready")
        v_ml_set = sem("v_ml_set")
        scores_done = sem("scores_done")
        scores_read = sem("scores_read")
        nsmax_set = sem("nsmax_set")
        exp_done = sem("exp_done")
        prob_ready = sem("prob_ready")
        prob_turned = sem("prob_turned")
        pT_set = sem("pT_set")
        pv_done = sem("pv_done")
        ya_hi_set = sem("ya_hi_set")
        ya_lo_set = sem("ya_lo_set")
        num_done = sem("num_done")
        num_read = sem("num_read")
        var_set = sem("var_set")
        lnr_set = sem("lnr_set")
        y_normed = sem("y_normed")
        ym_turned = sem("ym_turned")
        ym_hi_set = sem("ym_hi_set")
        ym_lo_set = sem("ym_lo_set")
        wout_done = sem("wout_done")
        merged = sem("merged")
        wo_half = sem("wo_half")
        x2_ready = sem("x2_ready")
        silu_f_done = sem("silu_f_done")
        hid_turned = sem("hid_turned")
        prod_done = sem("prod_done")
        a_hi_set = sem("a_hi_set")
        a_lo_set = sem("a_lo_set")
        ffn_out_done = sem("ffn_out_done")
        x3_ready = sem("x3_ready")
        gained = sem("gained")
        out0_ready = sem("out0_ready")
        out1_ready = sem("out1_ready")
        out2_ready = sem("out2_ready")
        stored = sem("stored")
        dve_step = sem("dve_step")

        block = ctx.enter_context(nc.Block())

        def chunk_source(c):
            if c < C_OUT:
                b, h = divmod(c, 2)
                if b < FEATURE_MAJOR:
                    return w_in_k[:, :, BLOCKS[b] + 256 * h:BLOCKS[b] + 256 * (h + 1)]
                return w_in_k[:, 4 * h:4 * h + 4, BLOCKS[b]:BLOCKS[b] + 512]
            if c < C_WO:
                w = woa_k if c < C_OUT + 2 else wom_k
                n = (c - C_OUT) % 2
                return w[:, :, 512 * n:512 * (n + 1)]
            if c < C_FFN:
                n, h = divmod(c - C_WO, 2)
                return wo_k[:, 4 * h:4 * h + 4, 512 * n:512 * (n + 1)]
            return (gate_k, up_k)[c - C_FFN][:, :, 0:256]

        def as_source(ap, src):
            return ap.rearrange("p (k n) -> p k n", n=src.shape[-1])

        @block.sync
        def _(sp):
            def load(c, src):
                if c >= RAW:
                    sp.wait_ge(lo_ready, c - RAW + 1)
                if c == 0:
                    sp.dma_start(as_source(w_raw[:, 0, 0:CH // 2], src), src[:, 0:4]).then_inc(first_half_loaded, 16)
                    sp.dma_start(as_source(w_raw[:, 0, CH // 2:CH], src), src[:, 4:8]).then_inc(chunk_loaded[0], 16)
                else:
                    sp.dma_start(as_source(w_raw[:, c % RAW, :], src), src).then_inc(chunk_loaded[c % RAW], 16)

            sp.dma_start(x_t[:, 0], x_d[:, 0]).then_inc(x_loaded[0], 16)
            sp.dma_start(x_t[:, 1], x_d[:, 1]).then_inc(x_loaded[1], 16)
            for c in range(C_FFN + 2):
                load(c, chunk_source(c))
                if c == 1:
                    with nc.allow_non_contiguous_dma(reason="eight gate columns"):
                        sp.dma_start(wif_raw, w_in_k[:, :, I_M:I_M + 2 * H_M]).then_inc(wif_loaded, 16)
                if c == 25:
                    sp.wait_ge(prob_turned, H_A // 2)
                    sp.dma_start(x_sb[:, :].rearrange("p (t n) -> p t n", t=T), x_d).then_inc(x_reloaded, 16)
                    sp.wait_ge(pv_done, H_A // 2)
                    sp.dma_start(gain_ffn, ffn_norm_g[0:1, :].to_broadcast([P, D])).then_inc(gain_ffn_loaded, 16)
                    sp.wait_ge(num_done, H_M)
                    sp.dma_start(gain_fin, final_norm_g.rearrange("(a n) -> a n", a=1).to_broadcast([P, D])
                                 ).then_inc(gain_fin_loaded, 16)
            with sp.Fori(0, (FG - 1) // 2) as i:
                for j in range(2):
                    c = C_FFN + 2 + 3 * j
                    srcs = (gate_k[:, :, bass.ds(i * 512 + 256 * (1 + j), 256)],
                            up_k[:, :, bass.ds(i * 512 + 256 * (1 + j), 256)],
                            down_k[:, bass.ds(i * 4 + 2 * j, 2), :])
                    for r, src in enumerate(srcs):
                        slot = (c + r) % RAW
                        sp.wait_ge(lo_ready, i * 6 + (c + r - RAW + 1))
                        n = 1024 if r == 2 else 256
                        sp.dma_start(w_raw[:, slot, :].rearrange("p (k n) -> p k n", n=n), src
                                     ).then_inc(chunk_loaded[slot], 16)
            c = C_FFN + 2 + 3 * (FG - 1)
            load(c, down_k[:, 2 * (FG - 1):2 * FG, :])
            for ready, t, half in ((out0_ready, 0, slice(0, D)), (out1_ready, 1, slice(0, 512)),
                                   (out2_ready, 1, slice(512, D))):
                sp.wait_ge(ready, 1)
                sp.dma_start(out_d[:, t, half], rb_t[:, t, half]).then_inc(stored, 16)
            sp.wait_ge(stored, 16 * 3)

        @block.gpsimd
        def _(pool):
            steps = [0]

            def link(ins):
                steps[0] += 1
                ins.then_inc(pool_step, 1)
                pool.wait_ge(pool_step, steps[0])

            def rsqrt(n):
                pool.wait_ge(sumsq_done, 2 * n + 1)
                link(nc.gpsimd.tensor_scalar(meansq[:, n:n + 1], sumsq[:, 2 * n:2 * n + 1], EPS, None, ALU.add))
                pool.wait_ge(sumsq_done, 2 * n + 2)
                link(nc.gpsimd.tensor_tensor(meansq[:, n:n + 1], meansq[:, n:n + 1],
                                             sumsq[:, 2 * n + 1:2 * n + 2], ALU.add))
                nc.gpsimd.tensor_tensor(rstd[:, n:n + 1], meansq[:, n:n + 1], minus_half[:, 0:1],
                                        ALU.pow).then_inc(rstd_done, 1)

            nc.gpsimd.memset(ones_row, 1.0).then_inc(ones_set, 1)
            nc.gpsimd.memset(minus_half[:, :], -0.5).then_inc(squares_warm, 1)
            link(nc.gpsimd.memset(ident[:, :], 0.0))
            nc.gpsimd.affine_select(out=ident[:, :], in_=ident[:, :], compare_op=ALU.not_equal, fill=1.0,
                                    base=0, pattern=[[-1, P]], channel_multiplier=1).then_inc(ident_set, 1)
            nc.gpsimd.memset(wif_pad, 0.0).then_inc(wif_zeroed, 1)
            for t in range(T):
                rsqrt(t)
            nc.gpsimd.memset(row_one, 1.0).then_inc(ones_set, 1)
            link(nc.gpsimd.memset(sel, 0.0))
            nc.gpsimd.affine_select(out=sel.rearrange("p (h n) -> p h n", h=H_M),
                                    in_=sel.rearrange("p (h n) -> p h n", h=H_M),
                                    compare_op=ALU.not_equal, fill=-1.0, base=0,
                                    pattern=[[-1, H_M], [0, P]], channel_multiplier=1).then_inc(sel_set, 1)
            link(nc.gpsimd.iota(dist[:, 0:128], pattern=[[1, 128]], base=0, channel_multiplier=-1,
                                allow_small_or_imprecise_dtypes=True))
            link(nc.gpsimd.iota(dist[:, 128:384], pattern=[[1, 256]], base=-128, channel_multiplier=-1,
                                allow_small_or_imprecise_dtypes=True))
            for h in range(H_A):
                slope = 2.0 ** (-8.0 * (h + 1) / H_A)
                ins = nc.gpsimd.tensor_scalar(alibi[:, h, :], dist, slope * D_A ** 0.5, None, ALU.mult)
            link(ins)
            for lo in (0, 256):
                part = alibi[:, :, lo:lo + 128]
                nc.gpsimd.affine_select(out=part, in_=part, compare_op=ALU.is_ge, fill=MASKED, base=0,
                                        pattern=[[0, H_A], [-1, 128]], channel_multiplier=1
                                        ).then_inc(alibi_set, 1)
            pool.wait_ge(w_exp_done, 2 * H_M)
            for lo in (0, 256):
                part = wm[:, :, lo:lo + 128]
                nc.gpsimd.affine_select(out=part, in_=part, compare_op=ALU.is_ge, fill=0.0, base=0,
                                        pattern=[[0, H_M], [1, 128]], channel_multiplier=-1
                                        ).then_inc(w_masked, 1)
            pool.wait_ge(var_set, H_M)
            link(nc.gpsimd.tensor_scalar(lnv[:, :], mv[:, :, 1], EPS, None, ALU.add))
            nc.gpsimd.tensor_tensor(lnr[:, :], lnv[:, :], minus_half[:, :], ALU.pow).then_inc(lnr_set, 1)
            for n in range(2, 6):
                rsqrt(n)

        @block.scalar
        def _(act):
            def split_hi(c):
                act.wait_ge(chunk_loaded[c % RAW], 16 * (c // RAW + 1))
                if c >= RING:
                    act.wait_ge(chunk_used, c - RING + 1)
                nc.scalar.activation(w_hi[:, slot_of(c), :], w_raw[:, c % RAW, :], ACT.Copy).then_inc(hi_ready, 1)

            def square(n, h, wait, value):
                act.wait_ge(wait, value)
                if n:
                    act.wait_ge(sumsq_done, 2 * n + h - 1)
                half = slice(512 * h, 512 * (h + 1))
                nc.scalar.activation(o_sb[:, half], x_t[:, n % 2, half], ACT.Square, scale=D ** -0.5,
                                     accum_out=sumsq[:, 2 * n + h:2 * n + h + 1]).then_inc(sumsq_done, 1)

            def turn_hi(e, t, banks):
                for b, bank in enumerate(banks):
                    act.wait_ge(turned, 2 * e + b + 1)
                    nc.scalar.activation(hT_hi[:, 4 * b:4 * b + 4, t * P:(t + 1) * P],
                                         bank.rearrange("p (k n) -> p k n", k=4), ACT.Copy).then_inc(hT_hi_set, 1)

            def tap3(c):
                b, h = divmod(c, 2)
                act.wait_ge(chunk_used, c + 1)
                if c == 0:
                    act.wait_ge(vcol_set, 1)
                for f in range(2):
                    ft = 4 * b + 2 * h + f
                    col = 4 + 3 * 8 + ft
                    ins = nc.scalar.activation(qk_m[:, ft, :], pp[:, 2 * (b % 2) + h, f * S:(f + 1) * S],
                                               ACT.Copy, scale=vcol[:, col:col + 1])
                ins.then_inc(tap3_done, 1)

            def copy_qk(c):
                b, h = divmod(c, 2)
                act.wait_ge(chunk_used, c + 1)
                ft = 4 * (b - 2) + 2 * h
                nc.scalar.activation(qk_a[:, ft:ft + 2, :],
                                     pp[:, 2 * (b % 2) + h, :].rearrange("p (f n) -> p f n", f=2),
                                     ACT.Copy).then_inc(proj_free[b % 2], 1)

            def read_block(b, dst, func):
                for t in range(T):
                    if t == 0:
                        act.wait_ge(tile0_done, b - FEATURE_MAJOR + 1)
                    else:
                        act.wait_ge(chunk_used, 2 * b + 2)
                    nc.scalar.activation(dst(t), pp[:, 2 * (b % 2) + t, :], func).then_inc(proj_free[b % 2], 1)

            def softmax_exp(p):
                act.wait_ge(nsmax_set, p + 1)
                for e in range(2):
                    for lo, hi, q in ((0, 128, 0), (128, 384, 1)):
                        n = 4 * p + 2 * e + q
                        part = prob[:, p % 2, e, lo:hi]
                        ins = nc.scalar.activation(part, part, ACT.Exp, bias=nsmax[:, n:n + 1],
                                                   scale=D_A ** -0.5, accum_out=ssum[:, n:n + 1])
                ins.then_inc(exp_done, 1)

            def copy_pT(p):
                act.wait_ge(prob_turned, p + 1)
                if p:
                    act.wait_ge(pv_done, p)
                else:
                    act.wait_ge(m_spread, 1)
                for e in range(2):
                    ins = nc.scalar.activation(pT[:, e, :], pa[:, 2 + e, 0:384], ACT.Copy)
                ins.then_inc(pT_set, 1)

            def ya_hi(p):
                act.wait_ge(pv_done, p + 1)
                nc.scalar.activation(yT_hi[:, p, :], pa[:, 0, 0:S], ACT.Copy).then_inc(ya_hi_set, 1)

            act.dma_start(gmix_row, mix_norm_g[0:1, :]).then_inc(gmix_loaded, 16)
            act.dma_start(vec_rows[0:4, :], mlstm_norm_g.rearrange("a (h p) -> (a h) p", p=P)).then_inc(vec_loaded, 16)
            act.dma_start(vec_rows[4:36, :], conv_qk.rearrange("a j (f p) -> (a j f) p", p=P)).then_inc(vec_loaded, 16)
            with nc.allow_non_contiguous_dma(reason="four biases"):
                act.dma_start(b_if[:, 0:1], b_igate.rearrange("a h -> h a")).then_inc(bif_loaded, 16)
                act.dma_start(b_if[:, 1:2], b_fgate.rearrange("a h -> h a")).then_inc(bif_loaded, 16)
            act.wait_ge(squares_warm, 1)
            nc.scalar.activation(sinv[:, 0:8], minus_half[:, :], ACT.Square)
            for t in range(T):
                square(t, 0, x_loaded[t], 16)
                square(t, 1, x_loaded[t], 16)
            act.wait_ge(first_half_loaded, 16)
            nc.scalar.activation(w_hi[:, 0, 0:CH // 2], w_raw[:, 0, 0:CH // 2], ACT.Copy).then_inc(first_half_hi, 1)
            turn_hi(0, 0, (pa[:, 0, :], pa[:, 1, :]))
            turn_hi(1, 1, (pp[:, 2, :], pp[:, 3, :]))
            act.wait_ge(chunk_loaded[0], 16)
            nc.scalar.activation(w_hi[:, 0, CH // 2:CH], w_raw[:, 0, CH // 2:CH], ACT.Copy).then_inc(hi_ready, 1)
            for c in range(1, AHEAD):
                split_hi(c)
            act.wait_ge(wif_padded, 2)
            nc.scalar.activation(wif_hi[:, :, :], wif_pad, ACT.Copy).then_inc(wif_hi_set, 1)

            for c in range(C_OUT):
                split_hi(c + AHEAD)
                if c == 2:
                    act.wait_ge(gate_rows_set, 1)
                    nc.scalar.activation(row_l, row_l, ACT.Exp).then_inc(exp1_done, 1)
                    act.wait_ge(exp1_done, 1)
                    nc.scalar.activation(row_l, row_l, ACT.Ln, bias=1.0).then_inc(log_done, 1)
                if c == 4:
                    act.wait_ge(scans_done, 1)
                    nc.scalar.activation(row_e, row_e, ACT.Exp, scale=-1.0).then_inc(exp_m_done, 1)
                    for n in range(4):
                        act.wait_ge(conv_step, 6 * (n + 1))
                        nc.scalar.activation(qk_m[:, 2 * n:2 * n + 2, :], qk_m[:, 2 * n:2 * n + 2, :],
                                             ACT.Silu).then_inc(silu_done, 1)
                if c == 6:
                    act.wait_ge(m_spread, 1)
                    act.wait_ge(rcol_set, 1)
                    act.wait_ge(alibi_set, 2)
                    for h in range(H_M):
                        neg_m = pa[:, 2 + h // 2, (h % 2) * S:(h % 2 + 1) * S]
                        nc.scalar.activation(wm[:, h, 0:S], neg_m, ACT.Exp, bias=rcol[:, h:h + 1]
                                             ).then_inc(w_exp_done, 1)
                        nc.scalar.activation(wm[:, h, S:384], neg_m[:, 128:256], ACT.Exp,
                                             bias=rcol[:, 4 + h:5 + h]).then_inc(w_exp_done, 1)
                if c in (10, 11):
                    softmax_exp(c - 10)
                if c == 12:
                    copy_pT(0)
                if c == 13:
                    ya_hi(0)
                    softmax_exp(2)
                if c == 14:
                    copy_pT(1)
                if c == 15:
                    ya_hi(1)
                    softmax_exp(3)
                    read_block(6, lambda t: o_t[:, t], ACT.Sigmoid)
                if c == 16:
                    copy_pT(2)
                if c == 17:
                    ya_hi(2)
                    copy_pT(3)
                if c == 18:
                    ya_hi(3)
                if c < 4:
                    tap3(c)
                elif c < 8:
                    copy_qk(c)
                elif c == 9:
                    read_block(4, lambda t: va[:, t], ACT.Copy)
                elif c in (16, 18, 20):
                    b = c // 2 - 1
                    dst = (ra_t, rb_t)[(b - 7) // 2]
                    read_block(b, lambda t: dst[:, t, ((b - 7) % 2) * 512:((b - 7) % 2 + 1) * 512], ACT.Sigmoid)
                if c == 20:
                    for b in range(2):
                        act.wait_ge(ym_turned, b + 1)
                        for f in range(2):
                            h = 2 * b + f
                            ins = nc.scalar.activation(yT_hi[:, 4 + h, :], pa[:, 2 + b, f * S:(f + 1) * S],
                                                       ACT.Copy, scale=vcol[:, h:h + 1])
                        ins.then_inc(ym_hi_set, 1)
            read_block(NB - 1, lambda t: rb_t[:, t, 512:1024], ACT.Sigmoid)
            for c in range(C_OUT + AHEAD, C_OUT + 7):
                split_hi(c)
            turn_hi(2, 0, (pa[:, 0, :], pa[:, 1, :]))
            split_hi(C_OUT + 7)
            split_hi(C_FFN)
            turn_hi(3, 1, (pp[:, 0, :], pp[:, 1, :]))
            square(2, 0, x2_ready, 1)
            split_hi(C_FFN + 1)
            square(2, 1, x2_ready, 2)
            split_hi(C_FFN + 2)
            turn_hi(4, 0, (pa[:, 0, :], pa[:, 1, :]))
            square(3, 0, x2_ready, 3)
            split_hi(C_FFN + 3)
            square(3, 1, x2_ready, 4)
            turn_hi(5, 1, (pp[:, 0, :], pp[:, 1, :]))
            split_hi(C_FFN + 4)
            split_hi(C_FFN + 5)
            act.wait_ge(chunk_used, C_FFN + 1)
            nc.scalar.activation(hid[:, 0, :], pa[:, 2, :], ACT.Silu).then_inc(silu_f_done, 1)
            split_hi(C_FFN + 6)
            act.wait_ge(hid_turned, 1)
            nc.scalar.activation(yT_hi[:, 0:2, :], pa[:, 2, :].rearrange("p (f n) -> p f n", f=2), ACT.Copy
                                 ).then_inc(a_hi_set, 1)
            split_hi(C_FFN + 7)

            def hidden(i, g):
                act.wait_ge(chunk_used, i * 6 + (C_FFN + 3 * g))
                if i is not FIRST:
                    act.wait_ge(a_lo_set, i * 2 + (g - 1))
                nc.scalar.activation(hid[:, g % 2, :], pa[:, g % 2, :], ACT.Silu).then_inc(silu_f_done, 1)
                act.wait_ge(prod_done, i * 2 + g + 1)
                if i is not FIRST:
                    act.wait_ge(chunk_used, i * 6 + (C_FFN + 3 * g - 1))
                nc.scalar.activation(yT_hi[:, 2 * (g % 2):2 * (g % 2) + 2, :],
                                     hid[:, g % 2, :].rearrange("p (f n) -> p f n", f=2), ACT.Copy
                                     ).then_inc(a_hi_set, 1)

            hidden(FIRST, 1)
            with act.Fori(1, (FG - 1) // 2) as i:
                for j in range(2):
                    c = C_FFN + 2 + 3 * j
                    for r in range(3):
                        act.wait_ge(chunk_loaded[(c + r) % RAW], i * 32 + 16 * ((c + r) // RAW + 1))
                        act.wait_ge(chunk_used, i * 6 + (c + r - RING + 1))
                        nc.scalar.activation(w_hi[:, slot_of(c + r), :], w_raw[:, (c + r) % RAW, :], ACT.Copy
                                             ).then_inc(hi_ready, 1)
                    hidden(i, j)
            split_hi(C_FFN + 2 + 3 * (FG - 1))
            hidden((FG - 1) // 2, 0)
            for n in (4, 5):
                square(n, 0, x3_ready, 2 * n - 7)
                square(n, 1, x3_ready, 2 * n - 6)
            act.wait_ge(gained, 1)
            act.wait_ge(rstd_done, 6)
            nc.scalar.activation(rb_t[:, 1, 512:1024], rb_t[:, 1, 512:1024], ACT.Copy, scale=rstd[:, 5:6]
                                 ).then_inc(out2_ready, 1)

        @block.vector
        def _(dve):
            steps = [0]

            def link(ins):
                steps[0] += 1
                ins.then_inc(dve_step, 1)
                dve.wait_ge(dve_step, steps[0])

            def split_lo(c):
                dve.wait_ge(hi_ready, c + 1)
                nc.vector.tensor_tensor(w_lo[:, slot_of(c), :], w_raw[:, c % RAW, :],
                                        w_hi[:, slot_of(c), :].bitcast(F32), ALU.subtract).then_inc(lo_ready, 1)

            def turn_lo(e, t, banks):
                for b, bank in enumerate(banks):
                    dve.wait_ge(hT_hi_set, 2 * e + b + 1)
                    part = (slice(None), slice(4 * b, 4 * b + 4), slice(t * P, (t + 1) * P))
                    nc.vector.tensor_tensor(hT_lo[part], bank.rearrange("p (k n) -> p k n", k=4),
                                            hT_hi[part].bitcast(F32), ALU.subtract).then_inc(hT_lo_set, 1)

            def conv(c):
                b, h = divmod(c, 2)
                dve.wait_ge(tap3_done, c + 1)
                for s in range(1, CONV):
                    for f in range(2):
                        ft = 4 * b + 2 * h + f
                        col = 4 + (CONV - 1 - s) * 8 + ft
                        n = 6 * c + 2 * (s - 1) + f
                        if s > 1:
                            dve.wait_ge(conv_step, n - 1)
                        ins = nc.vector.scalar_tensor_tensor(
                            out=qk_m[:, ft, s:S], in0=pp[:, 2 * (b % 2) + h, f * S:(f + 1) * S - s],
                            scalar=vcol[:, col:col + 1], in1=qk_m[:, ft, s:S], op0=ALU.mult, op1=ALU.add)
                        ins.then_inc(conv_step, 1)

            def score_w(h):
                dve.wait_ge(qk_m_done, h + 1)
                if h == 0:
                    dve.wait_ge(w_masked, 2)
                nc.vector.scalar_tensor_tensor(out=wm[:, h, :], in0=pa[:, h % 2, 0:384], scalar=D_M ** -0.5,
                                               in1=wm[:, h, :], op0=ALU.mult, op1=ALU.mult).then_inc(w_ready, 1)

            def score_max(p):
                dve.wait_ge(alibi_set, 2)
                if p >= 2:
                    dve.wait_ge(prob_turned, p - 1)
                for e in range(2):
                    dve.wait_ge(scores_done, 2 * p + e + 1)
                    for lo, hi, q in ((0, 128, 0), (128, 384, 1)):
                        n = 4 * p + 2 * e + q
                        ins = nc.vector.tensor_tensor_reduce(
                            out=prob[:, p % 2, e, lo:hi], in0=pa[:, 2 + e, lo:hi],
                            in1=alibi[:, 2 * p + e, lo:hi], scale=1.0, scalar=LOWEST, op0=ALU.add,
                            op1=ALU.max, accum_out=smax[:, n:n + 1])
                    ins.then_inc(scores_read, 1)
                dve.wait_ge(scores_read, 2 * p + 2)
                nc.vector.tensor_scalar(nsmax[:, 4 * p:4 * p + 4], smax[:, 4 * p:4 * p + 4], -D_A ** -0.5, None,
                                        ALU.mult).then_inc(nsmax_set, 1)

            def prob_scale(p):
                dve.wait_ge(exp_done, p + 1)
                link(nc.vector.reciprocal(sinv[:, 4 * p:4 * p + 4], ssum[:, 4 * p:4 * p + 4]))
                for e in range(2):
                    for lo, hi, q in ((0, 128, 0), (128, 384, 1)):
                        n = 4 * p + 2 * e + q
                        part = prob[:, p % 2, e, lo:hi]
                        ins = nc.vector.tensor_scalar(part, part, sinv[:, n:n + 1], None, ALU.mult)
                ins.then_inc(prob_ready, 1)

            def ya_lo(p):
                dve.wait_ge(ya_hi_set, p + 1)
                nc.vector.tensor_tensor(yT_lo[:, p, :], pa[:, 0, 0:S], yT_hi[:, p, :].bitcast(F32),
                                        ALU.subtract).then_inc(ya_lo_set, 1)

            def head_out(h):
                dve.wait_ge(num_done, h + 1)
                if h == 0:
                    dve.wait_ge(proj_free[0], 6)
                both = pa[:, 1, 0:2 * (D_M + 1)].rearrange("p (t n) -> p t n", t=T)
                link(nc.vector.scalar_tensor_tensor(
                    out=den[:, 2 * h:2 * h + 2], in0=both[:, :, D_M], scalar=-1.0,
                    in1=rcol[:, 8:16].rearrange("p (t h) -> p t h", t=T)[:, :, h], op0=ALU.mult, op1=ALU.max))
                link(nc.vector.tensor_tensor(den[:, 2 * h:2 * h + 2], both[:, :, D_M], den[:, 2 * h:2 * h + 2],
                                             ALU.max))
                link(nc.vector.reciprocal(dinv[:, 2 * h:2 * h + 2], den[:, 2 * h:2 * h + 2]))
                for t in range(T):
                    part = o_t[:, t, h * D_M:(h + 1) * D_M]
                    ins = nc.vector.scalar_tensor_tensor(
                        out=part, in0=both[:, t, 0:D_M], scalar=dinv[:, 2 * h + t:2 * h + t + 1], in1=part,
                        op0=ALU.mult, op1=ALU.mult)
                ins.then_inc(num_read, 1)
                dve.wait_ge(num_read, h + 1)
                for t in range(T):
                    ins = nc.vector.bn_stats(bn[:, 2 * h + t, :], o_t[:, t, h * D_M:(h + 1) * D_M])
                link(ins)
                for t in range(T):
                    ins = nc.vector.bn_aggr(mv[:, 2 * h + t, :], bn[:, 2 * h + t, :])
                ins.then_inc(var_set, 1)

            def merge(t, banks):
                dve.wait_ge(proj_free[0], 10)
                dve.wait_ge(proj_free[1], 8)
                if t == 0:
                    dve.wait_ge(wout_done, 1)
                else:
                    dve.wait_ge(chunk_used, C_OUT + 2)
                nc.vector.tensor_tensor(ra_t[:, t], banks[:, 0:2, :].rearrange("p b n -> p (b n)"), ra_t[:, t],
                                        ALU.mult)
                if t == 0:
                    dve.wait_ge(wout_done, 2)
                else:
                    dve.wait_ge(chunk_used, C_OUT + 4)
                link(nc.vector.tensor_tensor(rb_t[:, t], banks[:, 2:4, :].rearrange("p b n -> p (b n)"),
                                             rb_t[:, t], ALU.mult))
                nc.vector.tensor_tensor(ra_t[:, t], ra_t[:, t], rb_t[:, t], ALU.add).then_inc(merged, 1)

            def residual(t, n, bank, done, value, ready):
                half = slice(512 * n, 512 * (n + 1))
                dve.wait_ge(done, value)
                nc.vector.tensor_tensor(x_t[:, t, half], bank, x_t[:, t, half], ALU.add).then_inc(ready, 1)

            def norm(n, gain):
                t = n % 2
                dve.wait_ge(rstd_done, n + 1)
                for half in (slice(0, 512), slice(512, 1024)):
                    nc.vector.scalar_tensor_tensor(out=rb_t[:, t, half], in0=x_t[:, t, half],
                                                   scalar=rstd[:, n:n + 1], in1=gain[:, half],
                                                   op0=ALU.mult, op1=ALU.mult).then_inc(normed, 1)

            gain_mix = pa[:, 2:4, :].rearrange("p b n -> p (b n)")
            dve.wait_ge(gmix_spread, 1)
            norm(0, gain_mix)
            norm(1, gain_mix)
            turn_lo(0, 0, (pa[:, 0, :], pa[:, 1, :]))
            turn_lo(1, 1, (pp[:, 2, :], pp[:, 3, :]))
            for half, hi, lo in ((slice(0, CH // 2), first_half_hi, first_half_lo),
                                 (slice(CH // 2, CH), hi_ready, lo_ready)):
                dve.wait_ge(hi, 1)
                nc.vector.tensor_tensor(w_lo[:, 0, half], w_raw[:, 0, half], w_hi[:, 0, half].bitcast(F32),
                                        ALU.subtract).then_inc(lo, 1)
            dve.wait_ge(vec_turned, 1)
            nc.vector.tensor_copy(vcol[:, :], pp[:, 1, 0:36]).then_inc(vcol_set, 1)
            for c in range(1, AHEAD):
                split_lo(c)
                if c == 2:
                    dve.wait_ge(wif_loaded, 16)
                    dve.wait_ge(wif_zeroed, 1)
                    nc.vector.tensor_copy(wif_pad[:, :, 0:4], wif_raw[:, :, 0:4]).then_inc(wif_padded, 1)
                    nc.vector.tensor_copy(wif_pad[:, :, 32:36], wif_raw[:, :, 4:8]).then_inc(wif_padded, 1)
            dve.wait_ge(wif_hi_set, 1)
            nc.vector.tensor_tensor(wif_lo[:, :, :], wif_pad, wif_hi[:, :, :].bitcast(F32), ALU.subtract
                                    ).then_inc(wif_lo_set, 1)

            for c in range(C_OUT):
                split_lo(c + AHEAD)
                if c == 2:
                    dve.wait_ge(gates_done, 1)
                    dve.wait_ge(bif_loaded, 32)
                    nc.vector.tensor_scalar(row_i, pa[0:H_M, 0, 0:S], b_if[:, 0:1], None, ALU.add)
                    link(nc.vector.tensor_scalar(row_f, pa[32:32 + H_M, 0, 0:S], b_if[:, 1:2], None, ALU.add))
                    nc.vector.scalar_tensor_tensor(out=row_l, in0=row_f, scalar=-1.0, in1=row_f, op0=ALU.mult,
                                                   op1=ALU.min).then_inc(gate_rows_set, 1)
                if c == 3:
                    dve.wait_ge(log_done, 1)
                    dve.wait_ge(ones_set, 2)
                    link(nc.vector.scalar_tensor_tensor(out=row_f, in0=row_f, scalar=0.0, in1=row_l,
                                                        op0=ALU.min, op1=ALU.subtract))
                    link(nc.vector.tensor_tensor_scan(row_b, row_one, row_f, 0.0, ALU.mult, ALU.add))
                    link(nc.vector.tensor_tensor(row_i, row_i, row_b, ALU.subtract))
                    link(nc.vector.tensor_tensor_scan(row_m, row_one, row_i, 0.0, ALU.mult, ALU.max))
                    nc.vector.tensor_tensor(row_e, row_b, row_m, ALU.add).then_inc(scans_done, 1)
                if c == 6:
                    dve.wait_ge(cols_turned, 1)
                    nc.vector.tensor_copy(rcol[:, :], pa[:, 1, 0:16]).then_inc(rcol_set, 1)
                if c == 8:
                    score_w(0)
                    score_w(1)
                if c == 9:
                    score_w(2)
                    score_w(3)
                if c == 10:
                    score_max(0)
                if c == 11:
                    prob_scale(0)
                    score_max(1)
                if c == 12:
                    prob_scale(1)
                    dve.wait_ge(cols_turned, 1)
                    dve.wait_ge(m_spread, 1)
                    nc.vector.memset(vm[:, :, :, D_M:D_M + 1], 1.0).then_inc(v_ml_set, 1)
                    for t in range(T):
                        if t == 0:
                            dve.wait_ge(tile0_done, 2)
                        else:
                            dve.wait_ge(chunk_used, 2 * 5 + 2)
                        nc.vector.tensor_copy(vm[:, t, :, 0:D_M],
                                              pp[:, 2 + t, :].rearrange("p (h n) -> p h n", h=H_M)
                                              ).then_inc(proj_free[1], 1)
                if c == 13:
                    ya_lo(0)
                    score_max(2)
                if c == 14:
                    prob_scale(2)
                if c == 15:
                    ya_lo(1)
                    score_max(3)
                if c == 16:
                    prob_scale(3)
                    head_out(0)
                if c == 17:
                    ya_lo(2)
                    head_out(1)
                if c == 18:
                    ya_lo(3)
                    head_out(2)
                if c == 19:
                    head_out(3)
                    dve.wait_ge(lnr_set, 1)
                    dve.wait_ge(var_set, H_M)
                    for h in range(H_M):
                        for t in range(T):
                            part = o_t[:, t, h * D_M:(h + 1) * D_M]
                            n = 2 * h + t
                            ins = nc.vector.tensor_scalar(part, part, mv[:, n, 0:1], lnr[:, n:n + 1],
                                                          ALU.subtract, ALU.mult)
                    ins.then_inc(y_normed, 1)
                if c < 4:
                    conv(c)
                if c == 21:
                    for b in range(2):
                        dve.wait_ge(ym_hi_set, b + 1)
                        for f in range(2):
                            h = 2 * b + f
                            ins = nc.vector.scalar_tensor_tensor(
                                out=yT_lo[:, 4 + h, :], in0=pa[:, 2 + b, f * S:(f + 1) * S],
                                scalar=vcol[:, h:h + 1], in1=yT_hi[:, 4 + h, :].bitcast(F32),
                                op0=ALU.mult, op1=ALU.subtract)
                        ins.then_inc(ym_lo_set, 1)
            for c in range(C_OUT + AHEAD, C_OUT + 6):
                split_lo(c)
            merge(0, pa)
            split_lo(C_OUT + 6)
            turn_lo(2, 0, (pa[:, 0, :], pa[:, 1, :]))
            split_lo(C_OUT + 7)
            merge(1, pp)
            split_lo(C_FFN)
            turn_lo(3, 1, (pp[:, 0, :], pp[:, 1, :]))
            dve.wait_ge(x_reloaded, 16)
            dve.wait_ge(gain_ffn_loaded, 16)
            residual(0, 0, pa[:, 2, :], wo_half, 1, x2_ready)
            split_lo(C_FFN + 1)
            residual(0, 1, pa[:, 3, :], wo_half, 2, x2_ready)
            norm(2, gain_ffn)
            split_lo(C_FFN + 2)
            turn_lo(4, 0, (pa[:, 0, :], pa[:, 1, :]))
            residual(1, 0, pp[:, 2, :], chunk_used, C_WO + 2, x2_ready)
            residual(1, 1, pp[:, 3, :], chunk_used, C_WO + 4, x2_ready)
            norm(3, gain_ffn)
            split_lo(C_FFN + 3)
            turn_lo(5, 1, (pp[:, 0, :], pp[:, 1, :]))
            split_lo(C_FFN + 4)
            split_lo(C_FFN + 5)
            dve.wait_ge(silu_f_done, 1)
            dve.wait_ge(chunk_used, C_FFN + 2)
            nc.vector.tensor_tensor(hid[:, 0, :], pa[:, 0, :], hid[:, 0, :], ALU.mult).then_inc(prod_done, 1)
            split_lo(C_FFN + 6)
            dve.wait_ge(a_hi_set, 1)
            nc.vector.tensor_tensor(yT_lo[:, 0:2, :], pa[:, 2, :].rearrange("p (f n) -> p f n", f=2),
                                    yT_hi[:, 0:2, :].bitcast(F32), ALU.subtract).then_inc(a_lo_set, 1)
            split_lo(C_FFN + 7)

            def hidden(i, g):
                dve.wait_ge(silu_f_done, i * 2 + g + 1)
                dve.wait_ge(chunk_used, i * 6 + (C_FFN + 3 * g + 1))
                nc.vector.tensor_tensor(hid[:, g % 2, :], pa[:, 2 + g % 2, :], hid[:, g % 2, :], ALU.mult
                                        ).then_inc(prod_done, 1)
                dve.wait_ge(a_hi_set, i * 2 + g + 1)
                part = (slice(None), slice(2 * (g % 2), 2 * (g % 2) + 2), slice(None))
                nc.vector.tensor_tensor(yT_lo[part], hid[:, g % 2, :].rearrange("p (f n) -> p f n", f=2),
                                        yT_hi[part].bitcast(F32), ALU.subtract).then_inc(a_lo_set, 1)

            hidden(FIRST, 1)
            with dve.Fori(1, (FG - 1) // 2) as i:
                for j in range(2):
                    c = C_FFN + 2 + 3 * j
                    for r in range(3):
                        dve.wait_ge(hi_ready, i * 6 + (c + r + 1))
                        nc.vector.tensor_tensor(w_lo[:, slot_of(c + r), :], w_raw[:, (c + r) % RAW, :],
                                                w_hi[:, slot_of(c + r), :].bitcast(F32), ALU.subtract
                                                ).then_inc(lo_ready, 1)
                    hidden(i, j)
            split_lo(C_FFN + 2 + 3 * (FG - 1))
            hidden((FG - 1) // 2, 0)
            dve.wait_ge(gain_fin_loaded, 16)
            for t in range(T):
                for n in range(2):
                    residual(t, n, pp[:, 2 * t + n, :], ffn_out_done, 2 * t + n + 1, x3_ready)
                if t == 0:
                    dve.wait_ge(rstd_done, 5)
                    nc.vector.scalar_tensor_tensor(out=rb_t[:, 0], in0=x_t[:, 0], scalar=rstd[:, 4:5],
                                                   in1=gain_fin, op0=ALU.mult, op1=ALU.mult
                                                   ).then_inc(out0_ready, 1)
            dve.wait_ge(x3_ready, 4)
            nc.vector.tensor_tensor(rb_t[:, 1, 512:1024], x_t[:, 1, 512:1024], gain_fin[:, 512:1024], ALU.mult
                                    ).then_inc(gained, 1)
            dve.wait_ge(rstd_done, 6)
            nc.vector.scalar_tensor_tensor(out=rb_t[:, 1, 0:512], in0=x_t[:, 1, 0:512], scalar=rstd[:, 5:6],
                                           in1=gain_fin[:, 0:512], op0=ALU.mult, op1=ALU.mult
                                           ).then_inc(out1_ready, 1)

        @block.tensor
        def _(pe):
            mm = nc.tensor.matmul

            def feature_chunk(c, bank):
                s = slot_of(c)
                hi, lo = w_hi[:, s, :], w_lo[:, s, :]
                for f in range(2):
                    o = bank[:, f * S:(f + 1) * S]
                    for k in range(KT):
                        w = slice(k * 256 + f * P, k * 256 + (f + 1) * P)
                        mm(o, hi[:, w], hT_hi[:, k, :], start=(k == 0), stop=False)
                        mm(o, hi[:, w], hT_lo[:, k, :], start=False, stop=False)
                        ins = mm(o, lo[:, w], hT_hi[:, k, :], start=False, stop=(k == KT - 1))
                return ins

            def token_product(o, aT_hi, aT_lo, k, t, w, s, start, stop):
                tok = slice(t * P, (t + 1) * P)
                mm(o, aT_hi[:, k, tok], w_hi[:, s, w], start=start, stop=False)
                mm(o, aT_lo[:, k, tok], w_hi[:, s, w], start=False, stop=False)
                return mm(o, aT_hi[:, k, tok], w_lo[:, s, w], start=False, stop=stop)

            def turn(src, banks, halves=None):
                for b, bank in enumerate(banks):
                    if halves is not None:
                        pe.wait_ge(normed, halves + b + 1)
                    for k in range(4):
                        n = 4 * b + k
                        ins = nc.tensor.transpose(bank[:, k * P:(k + 1) * P], src[:, n * P:(n + 1) * P], ident[:, :])
                    ins.then_inc(turned, 1)

            def keep_warm(n):
                for _ in range(n):
                    nc.tensor.transpose(pp[:, 0, 0:P], ident[:, :], ident[:, :])

            pe.wait_ge(ident_set, 1)
            keep_warm(WARM_A)
            pe.wait_ge(ones_set, 1)
            pe.wait_ge(gmix_loaded, 16)
            for n in range(2):
                ins = mm(pa[:, 2 + n, :], ones_row, gmix_row[:, 512 * n:512 * (n + 1)], start=True, stop=True)
            ins.then_inc(gmix_spread, 1)
            keep_warm(WARM_B)
            turn(rb_t[:, 0], (pa[:, 0, :], pa[:, 1, :]), 0)
            turn(rb_t[:, 1], (pp[:, 2, :], pp[:, 3, :]), 2)
            pe.wait_ge(vec_loaded, 32)
            nc.tensor.transpose(pp[:, 1, 0:36], vec_rows, ident[0:36, 0:36]).then_inc(vec_turned, 1)

            def gates():
                pe.wait_ge(wif_lo_set, 1)
                for k in range(KT):
                    mm(pa[0:36, 0, 0:S], wif_hi[:, k, :], hT_hi[:, k, :], start=(k == 0), stop=False)
                    mm(pa[0:36, 0, 0:S], wif_hi[:, k, :], hT_lo[:, k, :], start=False, stop=False)
                    ins = mm(pa[0:36, 0, 0:S], wif_lo[:, k, :], hT_hi[:, k, :], start=False, stop=(k == KT - 1))
                ins.then_inc(gates_done, 1)

            def gate_columns():
                pe.wait_ge(scans_done, 1)
                pe.wait_ge(sel_set, 1)
                for h in range(H_M):
                    ins = mm(pa[:, 2 + h // 2, (h % 2) * S:(h % 2 + 1) * S], sel[:, h * P:(h + 1) * P], row_m,
                             start=True, stop=True)
                ins.then_inc(m_spread, 1)
                pe.wait_ge(exp_m_done, 1)
                for n, row in enumerate((row_i, row_e)):
                    for t in range(T):
                        ins = nc.tensor.transpose(pa[:, 1, 8 * n + 4 * t:8 * n + 4 * t + 4],
                                                  row[:, t * P:(t + 1) * P], ident[0:H_M, 0:H_M])
                ins.then_inc(cols_turned, 1)

            def mlstm_scores(h):
                if h == 0:
                    pe.wait_ge(silu_done, 4)
                    pe.wait_ge(rcol_set, 1)
                if h >= 2:
                    pe.wait_ge(w_ready, h - 1)
                q, k = qk_m[:, h, :], qk_m[:, H_M + h, :]
                mm(pa[:, h % 2, 0:S], k[:, 0:P], q, start=True, stop=True)
                mm(pa[:, h % 2, S:384], k[:, P:S], q[:, P:S], start=True, stop=True).then_inc(qk_m_done, 1)

            def scores(p):
                if p == 0:
                    pe.wait_ge(w_exp_done, 2 * H_M)
                    pe.wait_ge(proj_free[0], 2)
                    pe.wait_ge(proj_free[1], 2)
                if p == 1:
                    pe.wait_ge(scores_read, 2)
                if p >= 2:
                    pe.wait_ge(pT_set, p - 1)
                for e in range(2):
                    half = slice(e * D_A, (e + 1) * D_A)
                    q, k = qk_a[half, p, :], qk_a[half, 4 + p, :]
                    mm(pa[:, 2 + e, 0:P], q[:, 0:P], k[:, 0:P], start=True, stop=True)
                    mm(pa[:, 2 + e, P:384], q[:, P:S], k, start=True, stop=True).then_inc(scores_done, 1)

            def prob_turn(p):
                pe.wait_ge(prob_ready, p + 1)
                pe.wait_ge(scores_read, min(2 * p + 4, H_A))
                if p == 3:
                    pe.wait_ge(pT_set, 3)
                for e in range(2):
                    for n in range(3):
                        ins = nc.tensor.transpose(pa[:, 2 + e, n * P:(n + 1) * P],
                                                  prob[:, p % 2, e, n * P:(n + 1) * P], ident[:, :])
                ins.then_inc(prob_turned, 1)

            def pv(p):
                pe.wait_ge(pT_set, p + 1)
                if p:
                    pe.wait_ge(ya_lo_set, p)
                else:
                    pe.wait_ge(w_ready, H_M)
                    pe.wait_ge(proj_free[0], 4)
                for e in range(2):
                    half = slice(e * D_A, (e + 1) * D_A)
                    cols = slice((2 * p + e) * D_A, (2 * p + e + 1) * D_A)
                    mm(pa[half, 0, 0:S], va[:, 0, cols], pT[:, e, 0:S], start=True, stop=False)
                    ins = mm(pa[half, 0, P:S], va[:, 1, cols], pT[:, e, S:384], start=False, stop=True)
                ins.then_inc(pv_done, 1)

            def numerators(h):
                if h == 0:
                    pe.wait_ge(w_ready, H_M)
                    pe.wait_ge(v_ml_set, 1)
                    pe.wait_ge(proj_free[1], 4)
                else:
                    pe.wait_ge(num_read, h)
                n = D_M + 1
                mm(pa[:, 1, 0:n], wm[:, h, 0:P], vm[:, 0, h, :], start=True, stop=True)
                mm(pa[:, 1, n:2 * n], wm[:, h, P:S], vm[:, 0, h, :], start=True, stop=False)
                mm(pa[:, 1, n:2 * n], wm[:, h, S:384], vm[:, 1, h, :], start=False, stop=True).then_inc(num_done, 1)

            def ym_turn():
                pe.wait_ge(y_normed, 1)
                pe.wait_ge(pT_set, 4)
                for b in range(2):
                    for f in range(2):
                        for t in range(T):
                            h = 2 * b + f
                            ins = nc.tensor.transpose(pa[:, 2 + b, f * S + t * P:f * S + (t + 1) * P],
                                                      o_t[:, t, h * D_M:(h + 1) * D_M], ident[:, :])
                    ins.then_inc(ym_turned, 1)

            for c in range(C_OUT):
                b, h = divmod(c, 2)
                if c:
                    pe.wait_ge(lo_ready, c + 1)
                if c == 0:
                    for f in range(2):
                        for a, (w_part, x_part, first, second, xs) in enumerate((
                                (w_hi, hT_hi, first_half_hi, hi_ready, hT_hi_set),
                                (w_hi, hT_lo, first_half_hi, hi_ready, hT_lo_set),
                                (w_lo, hT_hi, first_half_lo, lo_ready, hT_hi_set))):
                            pe.wait_ge(xs, 4)
                            for k in range(KT):
                                if k % 4 == 0:
                                    pe.wait_ge(second if k else first, 1)
                                ins = mm(pp[:, 0, f * S:(f + 1) * S],
                                         w_part[:, 0, k * 256 + f * P:k * 256 + (f + 1) * P], x_part[:, k, :],
                                         start=(a == 0 and k == 0), stop=(a == 2 and k == KT - 1))
                    ins.then_inc(chunk_used, 1)
                elif b < FEATURE_MAJOR:
                    if b >= 2:
                        pe.wait_ge(conv_step, 6 * (c - 3))
                    if c == 1:
                        pe.wait_ge(vcol_set, 1)
                    feature_chunk(c, pp[:, 2 * (b % 2) + h, :]).then_inc(chunk_used, 1)
                else:
                    for t in range(T):
                        if h == 0:
                            pe.wait_ge(proj_free[b % 2], 2 * (b // 2 - 1) - 1 + t)
                        for k in range(4):
                            ins = token_product(pp[:, 2 * (b % 2) + t, :], hT_hi, hT_lo, 4 * h + k, t,
                                                slice(512 * k, 512 * (k + 1)), slot_of(c),
                                                h == 0 and k == 0, h == 1 and k == 3)
                        if h == 1 and t == 0:
                            ins.then_inc(tile0_done, 1)
                    ins.then_inc(chunk_used, 1)
                if c == 1:
                    gates()
                elif c == 5:
                    gate_columns()
                elif c == 7:
                    mlstm_scores(0)
                    mlstm_scores(1)
                elif c == 8:
                    mlstm_scores(2)
                    mlstm_scores(3)
                elif c in (9, 10):
                    scores(c - 9)
                elif c == 11:
                    prob_turn(0)
                elif c == 12:
                    pv(0)
                    scores(2)
                elif c == 13:
                    prob_turn(1)
                elif c == 14:
                    pv(1)
                    scores(3)
                elif c == 15:
                    prob_turn(2)
                    numerators(0)
                elif c == 16:
                    pv(2)
                    prob_turn(3)
                    numerators(1)
                elif c == 17:
                    pv(3)
                    numerators(2)
                elif c == 18:
                    numerators(3)
                elif c == 19:
                    ym_turn()

            for t in range(T):
                banks = (pa, pp)[t]
                if t == 1:
                    pe.wait_ge(proj_free[0], 10)
                    pe.wait_ge(proj_free[1], 8)
                for m in range(2):
                    if t == 0:
                        if m == 0:
                            pe.wait_ge(ya_lo_set, 4)
                            pe.wait_ge(num_read, H_M)
                        else:
                            pe.wait_ge(ym_lo_set, 2)
                    for n in range(2):
                        c = C_OUT + 2 * m + n
                        pe.wait_ge(lo_ready, c + 1)
                        for k in range(4):
                            ins = token_product(banks[:, 2 * m + n, :], yT_hi, yT_lo, 4 * m + k, t,
                                                slice(512 * k, 512 * (k + 1)), slot_of(c), k == 0, k == 3)
                        if t == 1:
                            ins.then_inc(chunk_used, 1)
                    if t == 0:
                        ins.then_inc(wout_done, 1)
                    elif m == 0:
                        pe.wait_ge(merged, 1)
                        turn(ra_t[:, 0], (pa[:, 0, :], pa[:, 1, :]))

            def out_product(t, banks):
                for n in range(2):
                    for h in range(2):
                        c = C_WO + 2 * n + h
                        pe.wait_ge(lo_ready, c + 1)
                        for k in range(4):
                            ins = token_product(banks[:, n, :], hT_hi, hT_lo, 4 * h + k, t,
                                                slice(512 * k, 512 * (k + 1)), slot_of(c),
                                                h == 0 and k == 0, h == 1 and k == 3)
                        if t == 1:
                            ins.then_inc(chunk_used, 1)
                    if t == 0:
                        ins.then_inc(wo_half, 1)
                    if n == 0:
                        if t == 0:
                            pe.wait_ge(merged, 2)
                            turn(ra_t[:, 1], (pp[:, 0, :], pp[:, 1, :]))
                        else:
                            turn(rb_t[:, 0], (pa[:, 0, :], pa[:, 1, :]), 4)

            pe.wait_ge(hT_lo_set, 6)
            out_product(0, pa[:, 2:4, :])
            pe.wait_ge(hT_lo_set, 8)
            out_product(1, pp[:, 2:4, :])

            for t in range(T):
                pe.wait_ge(hT_lo_set, 10 + 2 * t)
                for r in range(2):
                    pe.wait_ge(lo_ready, C_FFN + r + 1)
                    for k in range(KT):
                        ins = token_product(pa[:, 2 - 2 * r, t * 256:(t + 1) * 256], hT_hi, hT_lo, k, t,
                                            slice(256 * k, 256 * (k + 1)), slot_of(C_FFN + r),
                                            k == 0, k == KT - 1)
                        if t == 0 and r == 1 and k == 1:
                            turn(rb_t[:, 1], (pp[:, 0, :], pp[:, 1, :]), 6)
                    if t == 1:
                        ins.then_inc(chunk_used, 1)

            def down(a, s, t, k, start, stop):
                for n in range(2):
                    ins = token_product(pp[:, 2 * t + n, :], yT_hi, yT_lo, 2 * a + k, t,
                                        slice(1024 * k + 512 * n, 1024 * k + 512 * (n + 1)), s, start, stop)
                return ins

            def group(i, g):
                start = i is FIRST and g == 1
                c = C_FFN + 3 * g - 1
                for r in range(2):
                    pe.wait_ge(lo_ready, i * 6 + (c + r + 1))
                    if not start:
                        pe.wait_ge((silu_f_done, prod_done)[r], i * 2 + (g - 1))
                    feature_chunk(c + r, pa[:, 2 * r + g % 2, :]).then_inc(chunk_used, 1)
                    if start and r == 0:
                        pe.wait_ge(prod_done, 1)
                        for f in range(2):
                            for t in range(T):
                                ins = nc.tensor.transpose(
                                    pa[:, 2, f * S + t * P:f * S + (t + 1) * P],
                                    hid[:, 0, t * 256 + f * P:t * 256 + (f + 1) * P], ident[:, :])
                        ins.then_inc(hid_turned, 1)
                pe.wait_ge(lo_ready, i * 6 + (c + 3))
                pe.wait_ge(a_lo_set, i * 2 + g)
                for t in range(T):
                    for k in range(2):
                        ins = down((g - 1) % 2, slot_of(c + 2), t, k, start and k == 0, False)
                ins.then_inc(chunk_used, 1)

            group(FIRST, 1)
            group(FIRST, 2)
            with pe.Fori(1, (FG - 1) // 2) as i:
                group(i, 1)
                group(i, 2)
            c = C_FFN + 2 + 3 * (FG - 1)
            pe.wait_ge(lo_ready, c + 1)
            pe.wait_ge(a_lo_set, FG)
            for t in range(T):
                for n in range(2):
                    for k in range(2):
                        ins = token_product(pp[:, 2 * t + n, :], yT_hi, yT_lo, 2 * ((FG - 1) % 2) + k, t,
                                            slice(1024 * k + 512 * n, 1024 * k + 512 * (n + 1)), slot_of(c),
                                            False, k == 1)
                    ins.then_inc(ffn_out_done, 1)


_INS = ['x', 'mix_norm_g', 'w_in', 'conv_qk', 'b_igate', 'b_fgate', 'mlstm_norm_g', 'w_out_attn',
        'w_out_mlstm', 'w_o', 'ffn_norm_g', 'w_ffn_gate', 'w_ffn_up', 'w_ffn_down', 'final_norm_g']


def kernel(**inputs):
    import numpy as np
    import concourse.bacc as bacc
    from concourse.bass_utils import run_bass_kernel_spmd

    nc = bacc.Bacc("TRN2", target_bir_lowering=False, num_devices=1)
    arrays, args = {}, []
    for name in _INS:
        a = np.ascontiguousarray(inputs[name])
        arrays[f"in_{name}"] = a
        args.append(nc.dram_tensor(f"in_{name}", a.shape, mybir.dt.from_np(a.dtype), kind="ExternalInput").ap())
    args.append(nc.dram_tensor("out_x", (1, S, D), F32, kind="ExternalOutput").ap())
    build(nc, *args)
    return run_bass_kernel_spmd(nc, [arrays], core_ids=[0]).results[0]["out_x"]
```
